# Optimizing a Trainium2 kernel written in Bass

```python
import math
import jax, jax.numpy as jnp
from jax import lax
import numpy as np

D_MODEL = 1024
BATCH = 1
SEQ = 512
DEPTH = 2
DEC_BATCH = 8
DEC_SEQ = 8
PAST_LEN = 4096
PAGE_SIZE = 128

N_MIXERS = 2
N_MLSTM = (DEPTH + 1) // 2
N_S5 = DEPTH // 2
M_HEADS = 8
QK_DIM = D_MODEL // 2
V_DIM = D_MODEL
DK = QK_DIM // M_HEADS
DV = V_DIM // M_HEADS
MLSTM_CHUNK = 64
IN_COLS = 2 * QK_DIM + 2 * V_DIM + 2 * M_HEADS
S5_GROUP = 16
S5_GROUPS = D_MODEL // S5_GROUP
S5_STATE = 64
DT_MIN = 0.001
DT_MAX = 0.1
D_FF = 4 * D_MODEL
EPS = 1e-6

kernel_name = "mlstm_s5_hybrid_decode_step"

def rms_norm(x, g):
    xf = x.astype(jnp.float32)
    y = xf * lax.rsqrt(jnp.mean(xf * xf, axis=-1, keepdims=True) + EPS)
    return (y * g.astype(jnp.float32)).astype(x.dtype)

def sq_relu_mlp(x, w_up, w_down):
    h = jnp.square(jax.nn.relu(jnp.einsum('bld,df->blf', x, w_up)))
    return jnp.einsum('blf,fd->bld', h, w_down)

def mlstm_chunkwise(q, k, v, logi, logf, C0, n0, m0):
    B, L = q.shape[0], q.shape[1]
    cs = math.gcd(L, MLSTM_CHUNK)
    nc = L // cs

    def to_chunks(a):
        a = a.reshape((B, nc, cs) + a.shape[2:])
        return jnp.swapaxes(jnp.moveaxis(a, 1, 0), 2, 3)

    mask = jnp.tril(jnp.ones((cs, cs), dtype=bool))

    def step(carry, xs):
        C, n, m = carry
        qc, kc, vc, li, lf = xs
        b = jnp.cumsum(lf, axis=-1)
        logD = b[..., :, None] - b[..., None, :] + li[..., None, :]
        logD = jnp.where(mask, logD, -jnp.inf)
        inter = b + m[..., None]
        m_t = jnp.maximum(inter, jnp.max(logD, axis=-1))
        w_intra = jnp.exp(logD - m_t[..., None])
        w_inter = jnp.exp(inter - m_t)
        s = jnp.einsum('bhtd,bhsd->bhts', qc, kc) * w_intra
        num = (w_inter[..., None] * jnp.einsum('bhtd,bhde->bhte', qc, C)
               + jnp.einsum('bhts,bhse->bhte', s, vc))
        den = w_inter * jnp.einsum('bhtd,bhd->bht', qc, n) + jnp.sum(s, axis=-1)
        den = jnp.maximum(jnp.abs(den), jnp.exp(-m_t))
        h = num / den[..., None]
        m_new = m_t[..., -1]
        decay = jnp.exp(b[..., -1] + m - m_new)
        ws = jnp.exp(b[..., -1:] - b + li - m_new[..., None])
        C_new = decay[..., None, None] * C + jnp.einsum('bhs,bhsd,bhse->bhde', ws, kc, vc)
        n_new = decay[..., None] * n + jnp.einsum('bhs,bhsd->bhd', ws, kc)
        return (C_new, n_new, m_new), h

    xs = (to_chunks(q), to_chunks(k), to_chunks(v), to_chunks(logi), to_chunks(logf))
    (C, n, m), h = lax.scan(step, (C0, n0, m0), xs)
    h = jnp.moveaxis(jnp.swapaxes(h, 2, 3), 0, 1).reshape(B, L, M_HEADS, DV)
    return h, C, n, m

def mlstm_mixer(x, w_in, b_i, b_f, head_g, w_out, C0, n0, m0):
    B, L, _ = x.shape
    f32 = jnp.float32
    proj = jnp.einsum('bld,de->ble', x, w_in).astype(f32)
    q, k, v, o, gi, gf = jnp.split(
        proj, [QK_DIM, 2 * QK_DIM, 2 * QK_DIM + V_DIM, 2 * QK_DIM + 2 * V_DIM,
               2 * QK_DIM + 2 * V_DIM + M_HEADS], axis=-1)
    q = q.reshape(B, L, M_HEADS, DK)
    k = k.reshape(B, L, M_HEADS, DK) * (DK ** -0.5)
    v = v.reshape(B, L, M_HEADS, DV)
    logi = gi + b_i.astype(f32)
    logf = jax.nn.log_sigmoid(gf + b_f.astype(f32))
    h, C, n, m = mlstm_chunkwise(q, k, v, logi, logf,
                                 C0.astype(f32), n0.astype(f32), m0.astype(f32))
    h = h * lax.rsqrt(jnp.mean(h * h, axis=-1, keepdims=True) + EPS)
    h = h.reshape(B, L, V_DIM) * head_g.astype(f32) * jax.nn.sigmoid(o)
    out = jnp.einsum('ble,ed->bld', h.astype(x.dtype), w_out)
    return out, C, n, m

def s5_mixer(x, lam_re, lam_im, log_dt, b_re, b_im, c_re, c_im, d_skip, w_glu, h0_re, h0_im):
    B, L, _ = x.shape
    f32 = jnp.float32
    u = x.astype(f32).reshape(B, L, S5_GROUPS, S5_GROUP)
    dt = jnp.exp(log_dt.astype(f32))[:, None]
    lr, li = lam_re.astype(f32), lam_im.astype(f32)
    mag = jnp.exp(lr * dt)
    a_re, a_im = mag * jnp.cos(li * dt), mag * jnp.sin(li * dt)
    den = lr * lr + li * li
    z_re = a_re - 1.0
    coef_re = (z_re * lr + a_im * li) / den
    coef_im = (a_im * lr - z_re * li) / den
    br, bi = b_re.astype(f32), b_im.astype(f32)
    bb_re = coef_re[..., None] * br - coef_im[..., None] * bi
    bb_im = coef_re[..., None] * bi + coef_im[..., None] * br
    bu_re = jnp.einsum('blgc,gpc->blgp', u, bb_re)
    bu_im = jnp.einsum('blgc,gpc->blgp', u, bb_im)
    a_re_s = jnp.broadcast_to(a_re[None, None], (1, L, S5_GROUPS, S5_STATE))
    a_im_s = jnp.broadcast_to(a_im[None, None], (1, L, S5_GROUPS, S5_STATE))

    def combine(e1, e2):
        a1r, a1i, b1r, b1i = e1
        a2r, a2i, b2r, b2i = e2
        return (a1r * a2r - a1i * a2i, a1r * a2i + a1i * a2r,
                a2r * b1r - a2i * b1i + b2r, a2r * b1i + a2i * b1r + b2i)

    acr, aci, bcr, bci = lax.associative_scan(combine, (a_re_s, a_im_s, bu_re, bu_im), axis=1)
    h0r = h0_re.astype(f32)[:, None]
    h0i = h0_im.astype(f32)[:, None]
    h_re = acr * h0r - aci * h0i + bcr
    h_im = acr * h0i + aci * h0r + bci
    y = (jnp.einsum('gcp,blgp->blgc', c_re.astype(f32), h_re)
         - jnp.einsum('gcp,blgp->blgc', c_im.astype(f32), h_im)
         + d_skip.astype(f32).reshape(S5_GROUPS, S5_GROUP) * u)
    y = jax.nn.gelu(y.reshape(B, L, D_MODEL)).astype(x.dtype)
    ag = jnp.einsum('bld,de->ble', y, w_glu)
    a, g = jnp.split(ag, 2, axis=-1)
    out = a * jax.nn.sigmoid(g)
    return out, h_re[:, -1], h_im[:, -1]

def trunk(x, mC, mn, mm, sre, sim, p):
    new_C, new_n, new_m, new_re, new_im = [], [], [], [], []
    for layer in range(DEPTH):
        j = layer // N_MIXERS
        h = rms_norm(x, p['norm_mix_g'][layer])
        if layer % N_MIXERS == 0:
            out, C, n, m = mlstm_mixer(h, p['mlstm_w_in'][j], p['mlstm_b_i'][j], p['mlstm_b_f'][j],
                                       p['mlstm_head_norm_g'][j], p['mlstm_w_out'][j],
                                       mC[j], mn[j], mm[j])
            new_C.append(C)
            new_n.append(n)
            new_m.append(m)
        else:
            out, hr, hi = s5_mixer(h, p['s5_lambda_re'][j], p['s5_lambda_im'][j], p['s5_log_dt'][j],
                                   p['s5_b_re'][j], p['s5_b_im'][j], p['s5_c_re'][j], p['s5_c_im'][j],
                                   p['s5_d'][j], p['s5_w_glu'][j], sre[j], sim[j])
            new_re.append(hr)
            new_im.append(hi)
        x = x + out.astype(x.dtype)
        x = x + sq_relu_mlp(rms_norm(x, p['norm_ffn_g'][layer]),
                            p['ffn_w_up'][layer], p['ffn_w_down'][layer]).astype(x.dtype)
    y = rms_norm(x, p['norm_final_g'])
    return (y, jnp.stack(new_C), jnp.stack(new_n), jnp.stack(new_m),
            jnp.stack(new_re), jnp.stack(new_im))

def setup_inputs(seed: int = 0) -> dict:
    key = jax.random.key(seed)
    ks = jax.random.split(key, 32)
    f32 = jnp.float32
    nrm = lambda k, shape, s: jax.random.normal(k, shape, f32) * s
    lam_re = -0.5 + nrm(ks[0], (N_S5, S5_GROUPS, S5_STATE), 0.01)
    lam_im = (math.pi * jnp.arange(S5_STATE, dtype=f32))[None, None] + nrm(ks[1], (N_S5, S5_GROUPS, S5_STATE), 0.01)
    log_dt = jax.random.uniform(ks[2], (N_S5, S5_GROUPS), f32, math.log(DT_MIN), math.log(DT_MAX))
    b_f = jnp.linspace(3.0, 6.0, M_HEADS, dtype=f32)[None] + nrm(ks[3], (N_MLSTM, M_HEADS), 0.1)
    return {
        'x_prompt': nrm(ks[4], (BATCH, SEQ, D_MODEL), 1.0),
        'x_sample': nrm(ks[5], (DEC_BATCH, DEC_SEQ, D_MODEL), 1.0),
        'state_mlstm_C': nrm(ks[6], (N_MLSTM, DEC_BATCH, M_HEADS, DK, DV), 0.5),
        'state_mlstm_n': nrm(ks[7], (N_MLSTM, DEC_BATCH, M_HEADS, DK), 0.5),
        'state_mlstm_m': nrm(ks[8], (N_MLSTM, DEC_BATCH, M_HEADS), 0.5),
        'state_s5_re': nrm(ks[9], (N_S5, DEC_BATCH, S5_GROUPS, S5_STATE), 0.3),
        'state_s5_im': nrm(ks[10], (N_S5, DEC_BATCH, S5_GROUPS, S5_STATE), 0.3),
        'norm_mix_g': 1.0 + nrm(ks[11], (DEPTH, D_MODEL), 0.02),
        'norm_ffn_g': 1.0 + nrm(ks[12], (DEPTH, D_MODEL), 0.02),
        'norm_final_g': 1.0 + nrm(ks[13], (D_MODEL,), 0.02),
        'mlstm_w_in': nrm(ks[14], (N_MLSTM, D_MODEL, IN_COLS), D_MODEL ** -0.5),
        'mlstm_b_i': -1.0 + nrm(ks[15], (N_MLSTM, M_HEADS), 0.1),
        'mlstm_b_f': b_f,
        'mlstm_head_norm_g': 1.0 + nrm(ks[16], (N_MLSTM, V_DIM), 0.02),
        'mlstm_w_out': nrm(ks[17], (N_MLSTM, V_DIM, D_MODEL), V_DIM ** -0.5),
        's5_lambda_re': lam_re,
        's5_lambda_im': lam_im,
        's5_log_dt': log_dt,
        's5_b_re': nrm(ks[18], (N_S5, S5_GROUPS, S5_STATE, S5_GROUP), (2 * S5_GROUP) ** -0.5),
        's5_b_im': nrm(ks[19], (N_S5, S5_GROUPS, S5_STATE, S5_GROUP), (2 * S5_GROUP) ** -0.5),
        's5_c_re': nrm(ks[20], (N_S5, S5_GROUPS, S5_GROUP, S5_STATE), S5_STATE ** -0.5),
        's5_c_im': nrm(ks[21], (N_S5, S5_GROUPS, S5_GROUP, S5_STATE), S5_STATE ** -0.5),
        's5_d': nrm(ks[22], (N_S5, D_MODEL), 1.0),
        's5_w_glu': nrm(ks[23], (N_S5, D_MODEL, 2 * D_MODEL), D_MODEL ** -0.5),
        'ffn_w_up': nrm(ks[24], (DEPTH, D_MODEL, D_FF), D_MODEL ** -0.5),
        'ffn_w_down': nrm(ks[25], (DEPTH, D_FF, D_MODEL), D_FF ** -0.5),
    }

def reference(x_prompt, x_sample, state_mlstm_C, state_mlstm_n, state_mlstm_m, state_s5_re, state_s5_im,
              norm_mix_g, norm_ffn_g, norm_final_g, mlstm_w_in, mlstm_b_i, mlstm_b_f, mlstm_head_norm_g,
              mlstm_w_out, s5_lambda_re, s5_lambda_im, s5_log_dt, s5_b_re, s5_b_im, s5_c_re, s5_c_im,
              s5_d, s5_w_glu, ffn_w_up, ffn_w_down):
    params = dict(norm_mix_g=norm_mix_g, norm_ffn_g=norm_ffn_g, norm_final_g=norm_final_g,
                  mlstm_w_in=mlstm_w_in, mlstm_b_i=mlstm_b_i, mlstm_b_f=mlstm_b_f,
                  mlstm_head_norm_g=mlstm_head_norm_g, mlstm_w_out=mlstm_w_out,
                  s5_lambda_re=s5_lambda_re, s5_lambda_im=s5_lambda_im, s5_log_dt=s5_log_dt,
                  s5_b_re=s5_b_re, s5_b_im=s5_b_im, s5_c_re=s5_c_re, s5_c_im=s5_c_im,
                  s5_d=s5_d, s5_w_glu=s5_w_glu, ffn_w_up=ffn_w_up, ffn_w_down=ffn_w_down)
    f32 = jnp.float32
    bp = x_prompt.shape[0]
    z_C = jnp.zeros((N_MLSTM, bp, M_HEADS, DK, DV), f32)
    z_n = jnp.zeros((N_MLSTM, bp, M_HEADS, DK), f32)
    z_m = jnp.zeros((N_MLSTM, bp, M_HEADS), f32)
    z_s = jnp.zeros((N_S5, bp, S5_GROUPS, S5_STATE), f32)
    y_prompt, p_C, p_n, p_m, p_re, p_im = trunk(x_prompt, z_C, z_n, z_m, z_s, z_s, params)
    y_sample, s_C, s_n, s_m, s_re, s_im = trunk(x_sample, state_mlstm_C, state_mlstm_n, state_mlstm_m,
                                                state_s5_re, state_s5_im, params)
    return (y_prompt, y_sample, p_C, p_n, p_m, p_re, p_im, s_C, s_n, s_m, s_re, s_im)


_drawn_inputs = setup_inputs


def setup_inputs(seed=0):
    import zlib

    import numpy as np

    out = dict(_drawn_inputs(seed))
    spreads = {}
    factors = {'norm_final_g': 20.376,
     'mlstm_head_norm_g': 14.775,
     's5_lambda_re': 53.981,
     'norm_ffn_g': 4.716,
     's5_c_re': 8.0,
     's5_c_im': 8.0,
     's5_d': 4.923,
     's5_w_glu': 4.305}
    for name, (base, spread) in spreads.items():
        noise = np.random.default_rng([zlib.crc32(name.encode()), seed]).standard_normal(out[name].shape)
        drawn = base * np.exp(spread * noise) if base else spread * noise
        out[name] = __import__('jax').numpy.asarray(drawn.astype(out[name].dtype))
    for name, factor in factors.items():
        out[name] = (out[name] * factor).astype(out[name].dtype)
    return out
```

```python
from contextlib import ExitStack

import numpy as np

import concourse.bass as bass
from concourse import mybir

ALU = mybir.AluOpType
ACT = mybir.ActivationFunctionType
F32 = mybir.dt.float32
F32R = mybir.dt.float32r

P = 128
D = 1024
KT = D // P
B = 8
T = 8
TS = B * T
L = 512
N = TS + L
HN = N // 2
COLS = N // T
NB = L // P
H = 8
DK = 64
DV = 128
E1 = DV + 1
GATE_ROW = 96 + 16
FF = 4
G = 64
GC = 16
SP = 64
GP = G // 2
EPS = 1e-6
PAD = (T - 1) * GC
TAPS = PAD + T * GC
TWO_PI_HI = 6.28125
TWO_PI_LO = 0.0019353071795864769
MAGIC = 12582912.0

I_QKVO = 1
I_OUT = 25
I_FFN = (33, 113)
I_GLU = 97
HID0 = (8, 48)
N_SLABS = 177
V_MIX0, V_MIX1, V_FFN0, V_FFN1, V_FIN, V_HEAD, V_SKIP = range(7)


def build(nc, x_prompt, x_sample, st_C, st_n, st_m, st_re, st_im, g_mix, g_ffn, g_fin, w_in, b_i, b_f,
          g_head, w_out, lam_re, lam_im, log_dt, b_re, b_im, c_re, c_im, s5_d, w_glu, w_up, w_down,
          y_prompt, y_sample, p_C, p_n, p_m, p_re, p_im, s_C, s_n, s_m, s_re, s_im):
    d_taps = nc.dram_tensor("d_taps", (D, TAPS), F32, kind="Internal").ap()
    d_u = nc.dram_tensor("d_u", (D, T, COLS), F32, kind="Internal").ap()
    d_y = nc.dram_tensor("d_y", (D, T, COLS), F32, kind="Internal").ap()

    slab_in = w_in[0].rearrange("(k p) c -> p k c", p=P)
    slab_out = w_out[0].rearrange("(k p) c -> p k c", p=P)
    slab_glu = w_glu[0].rearrange("(k p) c -> p k c", p=P)
    slab_up = [w_up[l].rearrange("(k p) c -> p k c", p=P) for l in range(2)]
    slab_down = [w_down[l].rearrange("(f k p) c -> p f k c", p=P, k=KT) for l in range(2)]

    ctx = ExitStack()
    with ctx:
        def sb(name, shape, dt=F32, stack=None):
            return (stack or ctx).enter_context(nc.sbuf_tensor(name, shape, dt))

        x = sb("x", [P, KT, N])
        raw = sb("raw", [P, 2, KT, P])
        whi = sb("whi", [P, 2, KT, P], F32R)
        wlo = sb("wlo", [P, 2, KT, P], F32R)
        R = sb("R", [P, N])
        acc = sb("acc", [P, N])
        sqb = sb("sqb", [P, N])
        ident = sb("ident", [P, P])
        ones = sb("ones", [P, P])
        vec = sb("vec", [P, 7, KT])
        eps = sb("eps", [P, 1])
        s5s = sb("s5s", [P, 7, GP])
        cT = sb("cT", [P, 2, GP, GC])
        nT = sb("nT", [P, 32])
        nN = sb("nN", [P, 4, H])
        nP = sb("nP", [DK, H])
        dcy = sb("dcy", [P, H, 4])
        gs = sb("gs", [8, 32])
        fin = sb("fin", [P, 8])
        A_RE, A_IM, CF_RE, CF_IM, MAG8, COS8, SIN8 = range(7)
        M0, BI, BF, DEC, MPT = 0, 9, 10, 11, 20

        with ExitStack() as early:
            xtok = sb("xtok", [P, 5, D], stack=early)
            gw = sb("gw", [8, 7, N], stack=early)
        Q4 = xtok[:, 0, 0:N]
        LF, LI, AM, BC, MM, GT1, GT2 = range(7)
        hid_hi = sb("hid_hi", [P, KT, N], F32R)
        hid_lo = sb("hid_lo", [P, KT, N], F32R)

        xg_stack = ExitStack()
        xg_hi = sb("xg_hi", [P, KT, N], F32R, stack=xg_stack)
        xg_lo = sb("xg_lo", [P, KT, N], F32R, stack=xg_stack)
        with ExitStack() as mixer:
            qkvo = sb("qkvo", [P, 25, N], stack=mixer)
            with ExitStack() as lam:
                lg = sb("lg", [GP, 20, P], stack=lam)
                dt2 = sb("dt2", [GP, 2, 2], stack=lam)
                vrow = sb("vrow", [56, P], stack=lam)
                nrow = sb("nrow", [32, P], stack=lam)
                craw = sb("craw", [P, 2, KT, 2, SP], stack=lam)
            OT = sb("OT", [P, 5, E1], stack=mixer)
            Htok = sb("Htok", [P, 5, DV], stack=mixer)
            Qblk = sb("Qblk", [P, 320], stack=mixer)
            Kws = sb("Kws", [P, 2, 5, DK], stack=mixer)
            Kblk = sb("Kblk", [TS, 2, B, DK], stack=mixer)
            CP = sb("CP", [DK, 2, DV], stack=mixer)
            TK = sb("TK", [P, 5, P], stack=mixer)
            EX = sb("EX", [P, 5, 96], stack=mixer)
            SEL = sb("SEL", [8, H, P], stack=mixer)
            Msk = sb("Msk", [TS, TS], stack=mixer)
            MB = sb("MB", [TS, B], stack=mixer)
            st5 = sb("st5", [P, 8, 5], stack=mixer)
            Is = sb("Is", [TS, E1], stack=mixer)
        with ExitStack() as s5_mem:
            EC = sb("EC", [P, GP, SP], stack=s5_mem)
            ES = sb("ES", [P, GP, SP], stack=s5_mem)
            bb = sb("bb", [P, 2, GP, GC], stack=s5_mem)
            PW = sb("PW", [P, 3, T + 1, GP], stack=s5_mem)
            CA = sb("CA", [P, 2, GP, T + 1, GC], stack=s5_mem)
            CT = CA[:].rearrange("p r g j c -> p (r g j c)")
            srow = sb("srow", [P, 4, P], stack=s5_mem)
            prow = sb("prow", [2 * GP, P], stack=s5_mem)
            h0 = sb("h0", [P, 2, B, GP], stack=s5_mem)
            with ExitStack() as ffn_mem:
                rbuf = sb("rbuf", [P, N], stack=ffn_mem)
                tbuf = sb("tbuf", [P, N], stack=ffn_mem)
                qbuf = sb("qbuf", [P, N], stack=ffn_mem)
                braw = sb("braw", [P, 2, GP, GC], stack=ffn_mem)
                ptmp = sb("ptmp", [P, 2, N], stack=ffn_mem)
            rowsel = ptmp[:, 0, 0:11 * GC]
            with ExitStack() as s5_run:
                GS = sb("GS", [P, 2, 4, T * GC], stack=s5_run)
                gtmp = sb("gtmp", [P, 4, T * GC], stack=s5_run)
                rot = sb("rot", [P, 4, 4, SP], stack=s5_run)
                rho = sb("rho", [P, 4, SP], stack=s5_run)
                Hst = sb("Hst", [P, 2, 2, 4, COLS + 1], stack=s5_run)
                hP = sb("hP", [P, 2, GP], stack=s5_run)
                R2 = sb("R2", [P, COLS], stack=s5_run)
            with ExitStack() as glu_mem:
                gbuf = sb("gbuf", [P, N], stack=glu_mem)
                sbuf = sb("sbuf", [P, N], stack=glu_mem)
                tb2 = sb("tb2", [P, N], stack=glu_mem)
        E = qkvo[:, 16 - KT:16, :].rearrange("p a n -> p (a n)")[:, 0:2688].rearrange("p (s n) -> p s n", s=2)
        xg_stack.close()
        with ExitStack() as att:
            Vtok = sb("Vtok", [P, 5, H, E1], stack=att)
            Ktok = sb("Ktok", [P, 5, 4, P], stack=att)
            Cst = sb("Cst", [P, 2, 4, E1], stack=att)
        with ExitStack() as s5_a:
            U2 = sb("U2", [P, G, COLS], stack=s5_a)
            with ExitStack() as un_mem:
                unat = sb("unat", [P, KT, N], stack=un_mem)
            GT = sb("GT", [P, 2, 8, P], stack=s5_a)
            MT = sb("MT", [P, 2, 8, P], stack=s5_a)
            hN = sb("hN", [P, 2, B, GP], stack=s5_a)
        yn, yv = sqb, acc
        with ExitStack() as taps_mem:
            bblk = sb("bblk", [P, 2, GP, 2, GC], stack=taps_mem)
            ktap = sb("ktap", [P, KT, TAPS], stack=taps_mem)
        with ExitStack() as fin_mem:
            xf = sb("xf", [P, KT, N], stack=fin_mem)
            ybuf = sb("ybuf", [P, 2, D], stack=fin_mem)
        ps = ctx.enter_context(nc.psum_tensor("ps", [P, 8, 512], F32))

        def halves(ap):
            return ap.rearrange("p (n c) -> p n c", n=2)

        def slab_ps(s):
            return ps[:, 2 * s:2 * s + 2, 0:HN]

        names = """x_in vec_in lam_in craw_in nrow_in gate_in const_done xt_done x_ready sq_done acc_done xhi_done
            xg_ready whi_done w_ready slab_done stat_done rms_done R_ready scaled squared hhi_done
            hid_ready dve_step act_step pool_step vec_pe vec_ready lam_pe lam_act lam_dve craw_pe craw_ready
            gate_pe gate_act am_ready q4_clear q4_ready m_ready tk_pe tk_done ex_ready dec_pe
            dec_rhs att_const kv_done kv_act kv_dve osig_act osig_ready s_done arg_done exp_done p_done
            p_masked qblk_ready ncol_ready pv_done ot_act ot_ready ssq_done ms_ready rstd_ready htok_ready
            ht_done hf_ready kws_ready upa_done upb_done ca_done c_new n_pe n_rows
            fin_pe fin_act fin_ready b_in cc_done bb_done pool_pre taps_done kt_act taps_out u_ready u_out row_sel r2_pe r2_act r2_ready un_ready st5_in st5_pe h0_act gs_ready gt_done gt_ready v_done h_ready hin_ready hst_ready sy_done yev_ready y2_out yn_in dskip gel_done ssend_pe ssend_rows sig_done glu_done s5_set xf_ready yt_done y_act y_dve out_done""".split()
        sems = {n: ctx.enter_context(nc.semaphore(n)) for n in names}
        (x_in, vec_in, lam_in, craw_in, nrow_in, gate_in, const_done, xt_done, x_ready, sq_done, acc_done, xhi_done,
         xg_ready, whi_done, w_ready, slab_done, stat_done, rms_done, R_ready, scaled, squared, hhi_done,
         hid_ready, dve_step, act_step, pool_step, vec_pe, vec_ready, lam_pe, lam_act, lam_dve, craw_pe, craw_ready,
         gate_pe, gate_act, am_ready, q4_clear, q4_ready, m_ready, tk_pe, tk_done, ex_ready,
         dec_pe, dec_rhs, att_const, kv_done, kv_act, kv_dve, osig_act, osig_ready, s_done, arg_done, exp_done,
         p_done, p_masked, qblk_ready, ncol_ready, pv_done, ot_act, ot_ready, ssq_done, ms_ready, rstd_ready,
         htok_ready, ht_done, hf_ready, kws_ready, upa_done, upb_done, ca_done, c_new, n_pe, n_rows, fin_pe,
         fin_act, fin_ready, b_in, cc_done, bb_done, pool_pre, taps_done, kt_act, taps_out, u_ready, u_out, row_sel, r2_pe, r2_act, r2_ready, un_ready,
         st5_in, st5_pe, h0_act, gs_ready, gt_done, gt_ready, v_done, h_ready, hin_ready, hst_ready, sy_done,
         yev_ready, y2_out, yn_in, dskip, gel_done, ssend_pe, ssend_rows, sig_done, glu_done, s5_set, xf_ready, yt_done, y_act, y_dve, out_done) = (sems[n] for n in names)
        raw_in, ps_free, c_in, c_out, y_out, u2_in, mt_in = (
            [ctx.enter_context(nc.semaphore(f"{n}{s}")) for s in range(2)]
            for n in ("raw_in", "ps_free", "c_in", "c_out", "y_out", "u2_in", "mt_in"))

        class Steps:

            def __init__(self, eng, own):
                self.eng, self.own, self.n = eng, own, 0

            def link(self, ins):
                self.n += 1
                ins.then_inc(self.own, 1)
                self.eng.wait_ge(self.own, self.n)

        def load_slab(sp, base, j, src):
            s = base % 2
            if base >= 2:
                sp.wait_ge(w_ready, base - 1 + 2 * j)
            sp.dma_start(raw[:, s], src).then_inc(raw_in[s], 16)

        def split_hi(act, base, j):
            s = base % 2
            if base >= 2:
                act.wait_ge(slab_done, base - 1 + 2 * j)
            act.wait_ge(raw_in[s], 16 * (base // 2 + 1) + 16 * j)
            nc.scalar.activation(whi[:, s], raw[:, s], ACT.Copy).then_inc(whi_done, 1)

        def split_lo(dve, base, j):
            s = base % 2
            dve.wait_ge(whi_done, base + 1 + 2 * j)
            nc.vector.tensor_tensor(wlo[:, s], raw[:, s], whi[:, s].bitcast(F32),
                                    ALU.subtract).then_inc(w_ready, 1)

        def product(pe, base, j, rhs, ready=None):
            s = base % 2
            hi, lo = rhs
            pe.wait_ge(w_ready, base + 1 + 2 * j)
            if base >= 2:
                pe.wait_ge(ps_free[s], base // 2 + j)
            for k in range(KT):
                if ready:
                    pe.wait_ge(ready[0], ready[1] + k + 1)
                for n, (w, a) in enumerate(((whi, hi), (whi, lo), (wlo, hi))):
                    for c in range(2):
                        last = nc.tensor.matmul(ps[:, 2 * s + c, 0:HN], w[:, s, k, :],
                                                a[:, k, c * HN:(c + 1) * HN],
                                                start=(k == 0 and n == 0), stop=(k == KT - 1 and n == 2))
            last.then_inc(slab_done, 1)

        def stats(pe, stage):
            pe.wait_ge(acc_done, KT * (stage + 1))
            for c in range(2):
                last = nc.tensor.matmul(ps[:, 4 + c, 0:HN], ones[:], acc[:, c * HN:(c + 1) * HN],
                                        start=True, stop=True)
            last.then_inc(stat_done, 1)

        def rms(act, n):
            act.wait_ge(stat_done, n + 1)
            nc.scalar.activation(halves(R[:]), ps[:, 4:6, 0:HN], ACT.Sqrt, bias=eps[:, 0:1],
                                 scale=1.0 / D).then_inc(rms_done, 1)

        def inv_rms(dve, n):
            dve.wait_ge(rms_done, n + 1)
            nc.vector.reciprocal(R[:], R[:]).then_inc(R_ready, 1)
            dve.wait_ge(R_ready, n + 1)

        def gain(v, k):
            return vec[:, v, k:k + 1] if isinstance(k, int) else vec[:, v, bass.ds(k, 1)]

        def tile(a, k):
            return a[:, k] if isinstance(k, int) else a[:, bass.ds(k, 1), :].rearrange("p a n -> p (a n)")

        X_SLABS = {1: (I_OUT, 1), 2: (I_FFN[0] + 56, 1), 3: (I_GLU + 1, 2), 4: (I_FFN[1] + 56, 1)}

        def wait_x(eng, stage, q, j=0):
            if stage == 0:
                eng.wait_ge(x_ready, q + 1)
            else:
                base, step = X_SLABS[stage]
                base += step * q
                eng.wait_ge(ps_free[base % 2], base // 2 + 1 + step * j)

        def prep_hi(act, q, j, stage, n, v):
            wait_x(act, stage, q, j)
            k = q + 2 * j
            nc.scalar.activation(tile(xg_hi, k), tile(x, k), ACT.Identity,
                                 scale=gain(v, k)).then_inc(xhi_done, 1)

        def prep_lo(dve, k, n, v):
            dve.wait_ge(xhi_done, KT * n + 1 + k)
            nc.vector.scalar_tensor_tensor(tile(xg_lo, k), tile(x, k), gain(v, k), tile(xg_hi, k).bitcast(F32),
                                           ALU.mult, ALU.subtract).then_inc(xg_ready, 1)

        def square_sums(pool, stage):
            wait_x(pool, stage, 0)
            nc.gpsimd.tensor_tensor(acc[:], x[:, 0], x[:, 0], ALU.mult).then_inc(acc_done, 1)
            for k in range(1, KT):
                wait_x(pool, stage, k)
                pool.wait_ge(acc_done, KT * stage + k)
                nc.gpsimd.tensor_tensor(sqb[:], x[:, k], x[:, k], ALU.mult).then_inc(sq_done, 1)
                pool.wait_ge(sq_done, (KT - 1) * stage + k)
                nc.gpsimd.tensor_tensor(acc[:], acc[:], sqb[:], ALU.add).then_inc(acc_done, 1)

        YB = (0, 2, 6, 0, 2)
        OFF = [0, 512, 1024, 896]
        block = ctx.enter_context(nc.Block())

        @block.sync
        def _(sp):
            sp.dma_start(xtok[0:TS, 0, :], x_sample.rearrange("b t d -> (b t) d")).then_inc(x_in, 16)
            for i in range(NB):
                sp.dma_start(xtok[:, 1 + i, :], x_prompt[0, i * P:(i + 1) * P, :]).then_inc(x_in, 16)
            load_slab(sp, 0, 0, slab_in[:, :, 24 * P + 16 - P:24 * P + 16])
            load_slab(sp, 1, 0, slab_in[:, :, 0:P])
            for b4 in range(4):
                for b2 in range(2):
                    sp.dma_start(nrow[b4 * 8:b4 * 8 + 8, b2 * DK:(b2 + 1) * DK],
                                 st_n[0, 2 * b4 + b2]).then_inc(nrow_in, 16)
            with nc.allow_non_contiguous_dma(reason="80 numbers"):
                sp.dma_start(gs[:, M0:M0 + B], st_m[0].rearrange("b h -> h b")).then_inc(gate_in, 16)
                sp.dma_start(gs[:, BI:BI + 1], b_i.rearrange("a h -> h a")).then_inc(gate_in, 16)
                sp.dma_start(gs[:, BF:BF + 1], b_f.rearrange("a h -> h a")).then_inc(gate_in, 16)
            for ri, a in enumerate((c_re, c_im)):
                for dup in range(2):
                    sp.dma_start(craw[:, ri, :, dup, :],
                                 a[0].rearrange("(k g) c p -> (g c) k p", g=8)).then_inc(craw_in, 16)
            load_slab(sp, 2, 0, slab_in[:, :, P:2 * P])
            load_slab(sp, 3, 0, slab_in[:, :, 2 * P:3 * P])
            with sp.Fori(0, 10) as j:
                for q in range(2):
                    load_slab(sp, 4 + q, j, slab_in[:, :, bass.ds((3 + q) * P + j * (2 * P), P)])
            load_slab(sp, 24, 0, slab_in[:, :, 23 * P:24 * P])
            load_slab(sp, 25, 0, slab_out[:, :, 0:P])
            for c in range(1, 4):
                load_slab(sp, 25 + c, 0, slab_out[:, :, c * P:(c + 1) * P])

            def load_state(h):
                s = h % 2
                if h < 2:
                    sp.wait_ge(slab_done, 25)
                else:
                    sp.wait_ge(c_out[s], 16 * 3 * (h // 2))
                for b2 in range(2):
                    sp.dma_start(Cst[b2 * DK:(b2 + 1) * DK, s, :, 0:DV],
                                 st_C[0, b2::2, h].rearrange("b d e -> d b e")).then_inc(c_in[s], 16)

            load_state(0)
            load_state(1)
            sp.wait_ge(m_ready, 1)
            with nc.allow_non_contiguous_dma(reason="72 numbers"):
                sp.dma_start(s_m[0].rearrange("b h -> h b"), gs[:, MPT:MPT + B]).then_inc(out_done, 16)
                sp.dma_start(p_m[0].rearrange("b h -> h b"), gs[:, MPT + B:MPT + B + 1]).then_inc(out_done, 16)
            for h in range(H):
                s = h % 2
                sp.wait_ge(c_new, h + 1)
                for b2 in range(2):
                    sp.dma_start(s_C[0, b2::2, h].rearrange("b d e -> d b e"),
                                 Cst[b2 * DK:(b2 + 1) * DK, s, :, 0:DV]).then_inc(c_out[s], 16)
                sp.dma_start(p_C[0, 0, h], CP[:, s, :]).then_inc(c_out[s], 16)
                if h + 2 < H:
                    load_state(h + 2)
            sp.wait_ge(n_rows, 1)
            for b4 in range(4):
                for b2 in range(2):
                    sp.dma_start(s_n[0, 2 * b4 + b2], TK[b4 * 8:b4 * 8 + 8, 0, b2 * DK:(b2 + 1) * DK]).then_inc(out_done, 16)
            sp.dma_start(p_n[0, 0], TK[0:H, 1, 0:DK]).then_inc(out_done, 16)
            for c in range(4, KT):
                load_slab(sp, 25 + c, 0, slab_out[:, :, c * P:(c + 1) * P])

            def ffn_loads(l):
                up, down = I_FFN[l], I_FFN[l] + 8
                with sp.Fori(0, 4) as j:
                    for q in range(2):
                        load_slab(sp, up + q, j, slab_up[l][:, :, bass.ds(q * P + j * (2 * P), P)])
                with sp.Fori(0, FF - 1) as f:
                    with sp.Fori(0, 4) as j:
                        for q in range(2):
                            load_slab(sp, down + q, 8 * f + j, slab_down[l][:, bass.ds(f, 1), :, bass.ds(q * P + j * (2 * P), P)]
                                      .rearrange("p f k c -> p (f k) c"))
                    with sp.Fori(0, 4) as j:
                        for q in range(2):
                            load_slab(sp, up + 16 + q, 8 * f + j, slab_up[l][:, :, bass.ds((D + q * P) + f * D + j * (2 * P), P)])
                if l == 0:
                    for q in range(2):
                        load_slab(sp, down + 48 + q, 0, slab_down[l][:, FF - 1, :, q * P:(q + 1) * P])
                    return
                with sp.Fori(0, 4) as j:
                    for q in range(2):
                        load_slab(sp, down + 48 + q, j, slab_down[l][:, FF - 1, :, bass.ds(q * P + j * (2 * P), P)])

            sp.wait_ge(out_done, 16 * 11)
            for s in range(2):
                sp.wait_ge(c_out[s], 16 * 3 * 4)
            for ri, a in enumerate((b_re, b_im)):
                for g2 in range(2):
                    sp.dma_start(braw[g2 * SP:(g2 + 1) * SP, ri],
                                 a[0].rearrange("(a b) p c -> b p a c", b=2)[g2]).then_inc(b_in, 16)
            for hf in range(2):
                for ri, a in enumerate((st_re, st_im)):
                    sp.dma_start(srow[:, 2 * ri + hf, :],
                                 a[0].rearrange("b (a g) p -> (b a) (g p)", g=2)[hf * P:(hf + 1) * P]).then_inc(st5_in, 16)
            ffn_loads(0)

            def load_u(half):
                sp.wait_ge(u_out, 16 * 4 * (half + 1))
                g = slice(half * G // 2, (half + 1) * G // 2)
                for i in range(T):
                    sp.dma_start(U2[i * GC:(i + 1) * GC, g, :],
                                 d_u.rearrange("(g c) t b -> t c g b", c=GC)[T - 1 - i, :, g]).then_inc(u2_in[half], 16)

            for k in range(KT):
                if k < 6:
                    load_slab(sp, I_FFN[0] + 58 + k, 0, slab_down[0][:, FF - 1, :, (k + 2) * P:(k + 3) * P])
                else:
                    load_slab(sp, I_GLU + k - 6, 0, slab_glu[:, :, D * (7 - k):D * (7 - k) + P])
                if k == 4:
                    sp.wait_ge(taps_out, 16)
                    load_u(0)
                sp.wait_ge(u_ready, k + 1)
                sp.dma_start(d_u[k * P:(k + 1) * P].rearrange("p t b -> p (t b)"), unat[:, k]).then_inc(u_out, 16)
                if k == 3:
                    sp.wait_ge(kt_act, 2)
                    sp.dma_start(d_taps.rearrange("(k p) c -> p k c", p=P), ktap[:]).then_inc(taps_out, 16)
            load_u(1)

            def load_taps(k):
                s = k % 2
                if k >= 2:
                    sp.wait_ge(sy_done, k - 1)
                for i in range(T):
                    sp.dma_start(MT[i * GC:(i + 1) * GC, s],
                                 d_taps[k * P:(k + 1) * P, i * GC:i * GC + P].rearrange("(g c) m -> c g m", c=GC)).then_inc(mt_in[s], 16)

            load_taps(0)
            load_taps(1)
            for k in range(KT):
                if k + 2 < KT:
                    load_taps(k + 2)
                sp.wait_ge(yev_ready, k + 1)
                for i in range(T):
                    sp.dma_start(d_y[k * P:(k + 1) * P].rearrange("(g c) t b -> t c g b", c=GC)[i],
                                 U2[i * GC:(i + 1) * GC, 8 * k:8 * k + 8, :]).then_inc(y2_out, 16)
                sp.wait_ge(y2_out, 16 * T * (k + 1))
                if k:
                    sp.wait_ge(dskip, k)
                sp.dma_start(yn[:], d_y[k * P:(k + 1) * P].rearrange("p t b -> p (t b)")).then_inc(yn_in, 16)
            for i in range(2):
                load_slab(sp, I_GLU + 2 + i, 0, slab_glu[:, :, P + D * (1 - i):2 * P + D * (1 - i)])
            sp.wait_ge(ssend_rows, 1)
            for hf in range(2):
                for ri, a in enumerate((s_re, s_im)):
                    sp.dma_start(a[0].rearrange("b (a g) p -> (b a) (g p)", g=2)[hf * P:(hf + 1) * P],
                                 srow[:, 2 * ri + hf, :]).then_inc(out_done, 16)
            for ri, a in enumerate((p_re, p_im)):
                sp.dma_start(a[0, 0].rearrange("(a g) p -> a (g p)", g=2), prow[ri * GP:(ri + 1) * GP, :]).then_inc(out_done, 16)
            with sp.Fori(0, 6) as j:
                for i in range(2):
                    load_slab(sp, I_GLU + 4 + i, j, slab_glu[:, :, bass.ds(2 * P + D * (1 - i) + j * P, P)])
            ffn_loads(1)
            for i in range(5):
                s = i % 2
                sp.wait_ge(y_act, i + 1)
                sp.wait_ge(y_dve, i + 1)
                out = y_sample.rearrange("b t d -> (b t) d") if i == 0 else y_prompt[0, (i - 1) * P:i * P, :]
                sp.dma_start(out, ybuf[0:TS if i == 0 else P, s, :]).then_inc(y_out[s], 16)
            sp.wait_ge(y_out[0], 48)
            sp.wait_ge(y_out[1], 32)
            sp.wait_ge(out_done, 16 * 17)
            sp.wait_ge(c_out[0], 16 * 3 * 4)
            sp.wait_ge(c_out[1], 16 * 3 * 4)

        @block.gpsimd
        def _(pool):
            own = Steps(pool, pool_step)
            own.link(nc.gpsimd.memset(ident[:], 0.0))
            nc.gpsimd.affine_select(out=ident[:], in_=ident[:], compare_op=ALU.not_equal, fill=1.0, base=0,
                                    pattern=[[-1, P]], channel_multiplier=1).then_inc(const_done, 1)
            nc.gpsimd.memset(ones[:], 1.0)
            nc.gpsimd.memset(gs[:, 8:9], 0.0)
            nc.gpsimd.memset(eps[:], EPS).then_inc(const_done, 1)
            own.link(nc.gpsimd.memset(gw[:, AM, :], 1.0))
            nc.gpsimd.memset(gw[:, AM, 0:TS + 1:T], 0.0).then_inc(am_ready, 1)
            square_sums(pool, 0)
            pool.wait_ge(xt_done, KT)
            nc.gpsimd.memset(Q4, 0.0).then_inc(q4_clear, 1)
            pool.wait_ge(q4_clear, 1)
            pool.wait_ge(craw_ready, 3)
            own.link(nc.gpsimd.memset(SEL[:], 1.0))
            nc.gpsimd.affine_select(out=SEL[:], in_=SEL[:], compare_op=ALU.is_equal, fill=0.0, base=0,
                                    pattern=[[-1, H], [0, P]], channel_multiplier=1)
            nc.gpsimd.memset(Qblk[:], 0.0)
            nc.gpsimd.memset(OT[:], 0.0)
            nc.gpsimd.memset(TK[:], 0.0)
            own.link(nc.gpsimd.memset(MB[:], 1.0))
            own.link(nc.gpsimd.affine_select(out=MB[:], in_=MB[:], compare_op=ALU.is_ge, fill=0.0, base=0,
                                             pattern=[[-T, B]], channel_multiplier=1))
            own.link(nc.gpsimd.affine_select(out=MB[:], in_=MB[:], compare_op=ALU.is_ge, fill=0.0, base=T - 1,
                                             pattern=[[T, B]], channel_multiplier=-1))
            own.link(nc.gpsimd.tensor_copy(Msk[:].rearrange("s (b t) -> s b t", b=B),
                                           MB[:].unsqueeze(2).to_broadcast([TS, B, T])))
            nc.gpsimd.affine_select(out=Msk[:], in_=Msk[:], compare_op=ALU.is_ge, fill=0.0, base=0,
                                    pattern=[[1, TS]], channel_multiplier=-1).then_inc(att_const, 1)
            pool.wait_ge(slab_done, 25)
            nc.gpsimd.memset(Vtok[:, :, :, DV:E1], 1.0).then_inc(att_const, 1)
            pool.wait_ge(osig_act, 1)
            for h in range(H):
                nc.gpsimd.tensor_scalar(qkvo[:, 16 + h], qkvo[:, 16 + h], 1.0, 0.5, ALU.add, ALU.mult).then_inc(osig_ready, 1)

            def mask(h):
                e = E[:, h % 2]
                pool.wait_ge(p_done, h + 1)
                for j in range(NB):
                    blk = e[:, OFF[j]:OFF[j] + P]
                    nc.gpsimd.affine_select(out=blk, in_=blk, compare_op=ALU.is_ge, fill=0.0, base=0,
                                            pattern=[[1, P]], channel_multiplier=-1)
                nc.gpsimd.tensor_tensor(e[0:TS, 1280:1344], e[0:TS, 1280:1344], Msk[:], ALU.mult).then_inc(p_masked, 1)

            def n_column(h):
                pool.wait_ge(c_in[h % 2], 32 * (h // 2 + 1))
                nc.gpsimd.tensor_copy(Cst[:, h % 2, :, DV], nT[:].rearrange("p (b h) -> p b h", b=4)[:, :, h]).then_inc(ncol_ready, 1)

            n_column(0)
            mask(0)
            for h in range(H):
                if h + 1 < H:
                    mask(h + 1)
                pool.wait_ge(ms_ready, h + 1)
                nc.gpsimd.tensor_tensor(st5[:, 5, :], st5[:, 4, :], st5[:, 6, :], ALU.pow).then_inc(rstd_ready, 1)
                if h + 1 < H:
                    n_column(h + 1)
            square_sums(pool, 1)

            def cmul(out_re, out_im, a, b, tmp):
                t = nc.gpsimd.tensor_tensor
                t(tmp[0], a[0], b[0], ALU.mult)
                own.link(t(tmp[1], a[1], b[1], ALU.mult))
                own.link(t(out_re, tmp[0], tmp[1], ALU.subtract))
                t(tmp[0], a[0], b[1], ALU.mult)
                own.link(t(tmp[1], a[1], b[0], ALU.mult))
                own.link(t(out_im, tmp[0], tmp[1], ALU.add))

            pool.wait_ge(out_done, 16 * 11)
            for s in range(2):
                pool.wait_ge(c_out[s], 16 * 3 * 4)
            pool.wait_ge(hid_ready, 8)
            one = lambda n, w: s5s[:, n, :].unsqueeze(2).to_broadcast([P, GP, w])
            nc.gpsimd.tensor_copy(EC[:, :, 0], s5s[:, COS8, :])
            own.link(nc.gpsimd.tensor_copy(ES[:, :, 0], s5s[:, SIN8, :]))
            n = 1
            while n < SP:
                step = [t[:, :, n - 1:n].to_broadcast([P, GP, n]) for t in (EC, ES)]
                tmp = [CT[:, i * GP * 32:i * GP * 32 + GP * n].rearrange("p (g c) -> p g c", c=n) for i in range(2)]
                cmul(EC[:, :, n:2 * n], ES[:, :, n:2 * n], (EC[:, :, 0:n], ES[:, :, 0:n]), step, tmp)
                n *= 2
            nc.gpsimd.memset(PW[:, 0, 0, :], 1.0)
            nc.gpsimd.memset(PW[:, 1, 0, :], 0.0)
            nc.gpsimd.tensor_copy(PW[:, 0, 1, :], s5s[:, A_RE, :])
            own.link(nc.gpsimd.tensor_copy(PW[:, 1, 1, :], s5s[:, A_IM, :]))
            for m in (1, 2, 4):
                step = [PW[:, i, m:m + 1, :].to_broadcast([P, m, GP]) for i in range(2)]
                tmp = [ptmp[:, i, 0:m * GP].rearrange("p (m g) -> p m g", m=m) for i in range(2)]
                cmul(PW[:, 0, m + 1:2 * m + 1, :], PW[:, 1, m + 1:2 * m + 1, :],
                     (PW[:, 0, 1:m + 1, :], PW[:, 1, 1:m + 1, :]), step, tmp)
            own.link(nc.gpsimd.tensor_scalar(PW[:, 2], PW[:, 1], -1.0, None, ALU.mult))
            pool.wait_ge(b_in, 64)
            tmp = [ptmp[:, i, 0:GP * GC].rearrange("p (g c) -> p g c", g=GP) for i in range(2)]
            cmul(bb[:, 0], bb[:, 1], (one(CF_RE, GC), one(CF_IM, GC)), (braw[:, 0], braw[:, 1]), tmp)
            for k in range(KT):
                g = slice(4 * k, 4 * k + 4)
                c = [cT[:, ri, g, :].unsqueeze(2).to_broadcast([P, 4, T + 1, GC]) for ri in range(2)]
                a = [PW[:, v, :, g].rearrange("p j g -> p g j").unsqueeze(3).to_broadcast([P, 4, T + 1, GC]) for v in range(3)]
                tmp = [ptmp[:, i].rearrange("p (g j c) -> p g j c", g=4, c=GC) for i in range(2)]
                t = nc.gpsimd.tensor_tensor
                t(tmp[0], c[0], a[0], ALU.mult)
                own.link(t(tmp[1], c[1], a[1], ALU.mult))
                own.link(t(CA[:, 0, g], tmp[0], tmp[1], ALU.subtract))
                t(tmp[0], c[0], a[2], ALU.mult)
                own.link(t(tmp[1], c[1], a[0], ALU.mult))
                own.link(t(CA[:, 1, g], tmp[0], tmp[1], ALU.subtract))
            pool.wait_ge(slab_done, I_FFN[0] + 56)
            own.link(nc.gpsimd.memset(bblk[:], 0.0))
            own.link(nc.gpsimd.memset(ktap[:, :, 0:PAD], 0.0))
            for g2 in range(2):
                hf = slice(g2 * SP, (g2 + 1) * SP)
                last = nc.gpsimd.tensor_copy(bblk[hf, :, :, g2, :], bb[hf])
            last.then_inc(bb_done, 1)
            pool.wait_ge(bb_done, 1)
            own.link(nc.gpsimd.memset(rowsel, 0.0))
            nc.gpsimd.memset(rowsel[:, 7 * GC:8 * GC], 1.0).then_inc(row_sel, 1)

            def gains(k):
                g = slice(4 * k, 4 * k + 4)
                v = [bb[:, ri, g, :].unsqueeze(2).to_broadcast([P, 4, T, GC]) for ri in range(2)]
                a = [PW[:, ri, 0:T, g].rearrange("p j g -> p g j").unsqueeze(3).to_broadcast([P, 4, T, GC]) for ri in range(2)]
                re, im, tmp = (t.rearrange("p g (j c) -> p g j c", c=GC) for t in (GS[:, 0], GS[:, 1], gtmp[:]))
                t = nc.gpsimd.tensor_tensor
                if k:
                    pool.wait_ge(gt_done, k)
                t(re, v[0], a[0], ALU.mult)
                own.link(t(tmp, v[1], a[1], ALU.mult))
                own.link(t(re, re, tmp, ALU.subtract))
                t(im, v[0], a[1], ALU.mult)
                own.link(t(tmp, v[1], a[0], ALU.mult))
                t(im, im, tmp, ALU.add).then_inc(gs_ready, 1)

            pool.wait_ge(hid_ready, HID0[0] + 32)
            gains(0)
            square_sums(pool, 2)
            pool.wait_ge(r2_pe, 1)
            own.link(nc.gpsimd.memset(Hst[:, :, :, :, B:B + 1], 0.0))
            nc.gpsimd.memset(rho[:], 0.0).then_inc(s5_set, 1)

            for k in range(1, KT):
                gains(k)
            pool.wait_ge(h_ready, KT)
            pool.wait_ge(gt_done, KT)
            pool.wait_ge(gs_ready, KT)
            a8 = [PW[:, ri, T:T + 1, :].to_broadcast([P, B, GP]) for ri in range(2)]
            tmp = [GS[:, i // 2, 2 * (i % 2):2 * (i % 2) + 2, :].rearrange("p a b -> p (a b)").rearrange("p (b g) -> p b g", b=B)
                   for i in range(4)]
            cmul(tmp[2], tmp[3], a8, (h0[:, 0], h0[:, 1]), tmp)
            for ri in range(2):
                last = nc.gpsimd.tensor_tensor(hN[:, ri], hN[:, ri], tmp[2 + ri], ALU.add)
                if not ri:
                    own.link(last)
            last.then_inc(pool_pre, 1)
            pool.wait_ge(pool_pre, 1)
            square_sums(pool, 3)
            square_sums(pool, 4)

        @block.scalar
        def _(act):
            own = Steps(act, act_step)
            act.dma_start(lg[:, 0, :], lam_re[0].rearrange("(a b) p -> a (b p)", b=2)).then_inc(lam_in, 16)
            act.dma_start(lg[:, 1, :], lam_im[0].rearrange("(a b) p -> a (b p)", b=2)).then_inc(lam_in, 16)
            act.dma_start(dt2[:, 0, :], log_dt[0].rearrange("(a b) -> a b", b=2)).then_inc(lam_in, 16)
            for v, a in ((V_MIX0, g_mix), (V_FFN0, g_ffn), (V_HEAD, g_head), (V_SKIP, s5_d)):
                n = a.shape[0] * KT
                act.dma_start(vrow[v * KT:v * KT + n, :], a.rearrange("v (k p) -> (v k) p", p=P)).then_inc(vec_in, 16)
            act.dma_start(vrow[V_FIN * KT:(V_FIN + 1) * KT, :], g_fin.rearrange("(k p) -> k p", p=P)).then_inc(vec_in, 16)
            act.wait_ge(lam_in, 48)
            nc.scalar.activation(dt2[:, 1, :], dt2[:, 0, :], ACT.Exp).then_inc(lam_act, 1)
            act.wait_ge(lam_dve, 1)
            nc.scalar.activation(lg[:, 4, :], lg[:, 2, :], ACT.Exp)
            nc.scalar.activation(lg[:, 16, :], lg[:, 2, :], ACT.Exp, scale=float(T)).then_inc(lam_act, 1)
            act.wait_ge(lam_dve, 2)
            nc.scalar.activation(lg[:, 10:12, :], lg[:, 7:9, :], ACT.Sin).then_inc(lam_act, 1)
            split_hi(act, 0, 0)
            split_hi(act, 1, 0)
            act.wait_ge(vec_ready, 1)
            for k in range(KT):
                prep_hi(act, k, 0, 0, 0, V_MIX0)
            rms(act, 0)
            split_hi(act, 2, 0)
            split_hi(act, 3, 0)
            split_hi(act, 4, 0)
            act.wait_ge(gate_pe, 1)
            gz = halves(gw[:, GT1, :])
            act.wait_ge(gate_in, 48)
            own.link(nc.scalar.activation(gz, ps[0:8, 6:8, 0:HN], ACT.Abs, bias=gs[:, BF:BF + 1]))
            own.link(nc.scalar.activation(gw[:, GT1, :], gw[:, GT1, :], ACT.Exp, scale=-1.0))
            nc.scalar.activation(gw[:, GT1, :], gw[:, GT1, :], ACT.Ln, bias=ones[0:8, 0:1]).then_inc(gate_act, 1)
            act.wait_ge(m_ready, 1)
            nc.scalar.activation(gs[:, DEC:DEC + B], gs[:, DEC:DEC + B], ACT.Exp).then_inc(gate_act, 1)
            with act.Fori(0, 10) as j:
                for q in range(2):
                    split_hi(act, 5 + q, j)
            split_hi(act, 25, 0)
            split_hi(act, 26, 0)
            act.wait_ge(tk_pe, 1)
            act.wait_ge(att_const, 1)
            nc.scalar.activation(TK[0:TS, 0, :], ps[0:TS, 4, 0:P], ACT.Copy)
            own.link(nc.scalar.activation(TK[:, 1:5, :], ps[:, 5, :].rearrange("p (i c) -> p i c", i=NB), ACT.Copy))
            nc.scalar.activation(EX[:], TK[:, :, 32:P], ACT.Exp).then_inc(ex_ready, 1)
            own.link(nc.scalar.activation(dcy[0:DK], ps[0:DK, 6, 0:64].rearrange("p (h b c) -> p h b c", h=H, c=2)[:, :, :, 0], ACT.Copy))
            nc.scalar.activation(dcy[DK:P], ps[DK:P, 6, 0:64].rearrange("p (h b c) -> p h b c", h=H, c=2)[:, :, :, 1],
                                 ACT.Copy).then_inc(ex_ready, 1)
            act.wait_ge(ps_free[1], 12)
            act.wait_ge(ps_free[0], 13)
            nc.scalar.activation(qkvo[:, 16:24, :], qkvo[:, 16:24, :], ACT.Tanh, scale=0.5).then_inc(osig_act, 1)
            for i in range(0, 12, 2):
                act.wait_ge(kv_done, i + 1)
                r = 2 * (i % 4)
                if i < 4:
                    nc.scalar.activation(Ktok[:, 1:5, i, :], ps[:, r, :].rearrange("p (i c) -> p i c", i=NB), ACT.Copy)
                    nc.scalar.activation(Ktok[0:TS, 0, i, :], ps[0:TS, r + 1, 0:P], ACT.Copy).then_inc(kv_act, 1)
                else:
                    nc.scalar.activation(Vtok[:, 1:5, i - 4, 0:DV], ps[:, r, :].rearrange("p (i c) -> p i c", i=NB), ACT.Copy)
                    nc.scalar.activation(Vtok[0:TS, 0, i - 4, 0:DV], ps[0:TS, r + 1, 0:P], ACT.Copy).then_inc(kv_act, 1)

            def exps(h):
                e = E[:, h % 2]
                act.wait_ge(arg_done, h + 1)
                nc.scalar.activation(e[:, 0:1280], e[:, 0:1280], ACT.Exp)
                nc.scalar.activation(e[0:TS, 1280:1344], e[0:TS, 1280:1344], ACT.Exp).then_inc(exp_done, 1)

            def head_hi(h):
                act.wait_ge(hf_ready, h + 1)
                nc.scalar.activation(hid_hi[:, h], qkvo[:, 16 + h], ACT.Copy).then_inc(hhi_done, 1)

            exps(0)
            for h in range(H):
                if h + 1 < H:
                    exps(h + 1)
                if h:
                    head_hi(h - 1)
                act.wait_ge(pv_done, h + 1)
                if h:
                    act.wait_ge(htok_ready, h)
                nc.scalar.activation(OT[:, 1:4, :], ps[:, 4, 0:3 * E1].rearrange("p (i c) -> p i c", i=3), ACT.Copy)
                nc.scalar.activation(OT[:, 4, :], ps[:, 5, 0:E1], ACT.Copy)
                nc.scalar.activation(Is[:], ps[0:TS, 5, 2 * E1:3 * E1], ACT.Copy, scale=EX[0:TS, 0, 64 + h:65 + h]).then_inc(ot_act, 1)
                act.wait_ge(ot_ready, h + 1)
                if h:
                    act.wait_ge(ht_done, h)
                for i in range(5):
                    last = nc.scalar.activation(Htok[:, i, :], OT[:, i, 0:DV], ACT.Square, accum_out=st5[:, 2, i:i + 1])
                last.then_inc(ssq_done, 1)
            head_hi(H - 1)
            act.wait_ge(n_pe, 1)
            nc.scalar.activation(TK[0:32, 0, :], ps[0:32, 6, 256:384], ACT.Copy)
            nc.scalar.activation(TK[0:H, 1, 0:DK], ps[0:H, 7, 0:DK], ACT.Copy).then_inc(n_rows, 1)
            with act.Fori(0, 4) as j:
                for q in range(2):
                    prep_hi(act, q, j, 1, 1, V_FFN0)
                    split_hi(act, 27 + q, j)

            def up_act(base, j, e, n):
                s = base % 2
                act.wait_ge(slab_done, base + 1 + 2 * j)
                nc.scalar.activation(halves(rbuf[:]), slab_ps(s), ACT.Relu).then_inc(ps_free[s], 1)
                split_hi(act, base + 2, j)
                act.wait_ge(scaled, 32 * n + 1 + e)
                nc.scalar.activation(qbuf[:], tbuf[:], ACT.Square).then_inc(squared, 1)
                act.wait_ge(squared, 32 * n + 1 + e)
                return nc.scalar.activation

            def ffn_act(l):
                up, down = I_FFN[l], I_FFN[l] + 8
                rms(act, 1 + 2 * l)
                hid0 = HID0[l]

                def tile_up(base, j, e, k):
                    up_act(base, j, e, l)
                    nc.scalar.activation(tile(hid_hi, k), qbuf[:], ACT.Copy).then_inc(hhi_done, 1)

                with act.Fori(0, 4) as j:
                    for q in range(2):
                        tile_up(up + q, j, q + 2 * j, q + 2 * j)
                with act.Fori(0, FF - 1) as f:
                    with act.Fori(0, 4) as j:
                        for q in range(2):
                            split_hi(act, down + 2 + q, 8 * f + j)
                    with act.Fori(0, 4) as j:
                        for q in range(2):
                            tile_up(up + 16 + q, 8 * f + j, 8 + q + 8 * f + 2 * j, q + 2 * j)
                if l == 0:
                    for q in range(3):
                        split_hi(act, down + 50 + q, 0)
                    act.wait_ge(taps_done, 1)
                    nc.scalar.activation(h0[:].rearrange("p r b g -> p (r b g)"), ps[:, 4, :], ACT.Copy).then_inc(h0_act, 1)
                    for r in range(2):
                        nc.scalar.activation(ktap[:, 4 * r:4 * r + 4, PAD:TAPS], ps[:, 6 + r, :].rearrange("p (k c) -> p k c", k=4),
                                             ACT.Copy).then_inc(kt_act, 1)
                    for q in range(3, KT):
                        split_hi(act, down + 50 + q, 0)
                    return
                with act.Fori(0, 3) as j:
                    for q in range(2):
                        split_hi(act, down + 50 + q, j)

            act.wait_ge(out_done, 16 * 11)
            for s in range(2):
                act.wait_ge(c_out[s], 16 * 3 * 4)
            ffn_act(0)

            def gains_out(k):
                s = k % 2
                act.wait_ge(gt_done, k + 1)
                if k >= 2:
                    act.wait_ge(v_done, k - 1)
                elif k == 0:
                    act.wait_ge(u_out, 16 * 4)
                r = 2 * s
                nc.scalar.activation(GT[:, s].rearrange("p (r q) c -> p r (q c)", r=2), ps[:, r:r + 2, :], ACT.Copy).then_inc(gt_ready, 1)

            def gelu(k):
                act.wait_ge(dskip, k + 1)
                nc.scalar.activation(yv[:], yv[:], ACT.Gelu_apprx_tanh).then_inc(gel_done, 1)
                act.wait_ge(gel_done, k + 1)
                nc.scalar.activation(hid_hi[:, k], yv[:], ACT.Copy).then_inc(hhi_done, 1)

            gains_out(0)
            act.wait_ge(r2_pe, 1)
            nc.scalar.activation(R2[:], ps[:, 6, 0:COLS], ACT.Sqrt, bias=eps[:, 0:1], scale=1.0 / D).then_inc(r2_act, 1)
            rms(act, 2)
            for i in range(KT + 3):
                if i + 1 < KT:
                    gains_out(i + 1)
                if 0 <= i - 1 < KT:
                    k = i - 1
                    act.wait_ge(sy_done, k + 1)
                    nc.scalar.activation(U2[:, 8 * k:8 * k + 8, :].rearrange("p (q a) b -> p a q b", a=2),
                                         ps[:, 6:8, 0:4 * COLS].rearrange("p a (q b) -> p a q b", q=4),
                                         ACT.Copy).then_inc(yev_ready, 1)
                if i >= 3:
                    gelu(i - 3)
            act.wait_ge(ssend_pe, 1)
            nc.scalar.activation(srow[:].rearrange("p a b -> p (a b)"), ps[:, 4, :], ACT.Copy)
            nc.scalar.activation(prow[:], ps[0:2 * GP, 5, 0:P], ACT.Copy).then_inc(ssend_rows, 1)
            with act.Fori(0, 4) as j:
                for q in range(2):
                    base = I_GLU + 2 * q
                    act.wait_ge(slab_done, base + 1 + 4 * j)
                    act.wait_ge(ps_free[0], I_GLU // 2 + 1 + q + 2 * j)
                    nc.scalar.activation(halves(gbuf[:]), slab_ps(1), ACT.Tanh, scale=0.5).then_inc(ps_free[1], 1)
                    split_hi(act, base + 2, 2 * j)
                    split_hi(act, base + 3, 2 * j)
                    prep_hi(act, q, j, 3, 2, V_FFN1)
            ffn_act(1)
            for k in range(KT):
                wait_x(act, 4, k)
                nc.scalar.activation(xf[:, k], x[:, k], ACT.Identity, scale=gain(V_FIN, k)).then_inc(xf_ready, 1)
            act.wait_ge(fin_pe, 1)
            nc.scalar.activation(fin[0:TS, 0:1], ps[0:TS, 4, 0:1], ACT.Sqrt, bias=eps[0:TS, 0:1], scale=1.0 / D)
            nc.scalar.activation(fin[:, 1:5], ps[:, 4, 2:10:2], ACT.Sqrt, bias=eps[:, 0:1], scale=1.0 / D).then_inc(fin_act, 1)
            act.wait_ge(fin_ready, 1)
            for i in range(5):
                n = TS if i == 0 else P
                act.wait_ge(yt_done, i + 1)
                if i >= 2:
                    act.wait_ge(y_out[i % 2], 16 * (i // 2))
                nc.scalar.activation(ybuf[0:n, i % 2, 0:512], ps[0:n, YB[i], :], ACT.Copy, scale=fin[0:n, i:i + 1]).then_inc(y_act, 1)

        @block.vector
        def _(dve):
            own = Steps(dve, dve_step)
            V = nc.vector
            lr, li, lrdt, lidt, mag, t6, t9, t19 = (lg[:, n, :] for n in (0, 1, 2, 3, 4, 6, 9, 19))
            dve.wait_ge(lam_act, 1)
            dtb = dt2[:, 1, :].unsqueeze(2).to_broadcast([GP, 2, SP])
            for r in range(2):
                last = V.tensor_tensor(lg[:, 2 + r, :].rearrange("a (b p) -> a b p", b=2),
                                       lg[:, r, :].rearrange("a (b p) -> a b p", b=2), dtb, ALU.mult)
            last.then_inc(lam_dve, 1)
            dve.wait_ge(lam_dve, 1)
            for r, shift in ((7, 0.0), (8, 0.25)):
                own.link(V.tensor_scalar(t6, lidt, 1.0 / (2 * np.pi), shift, ALU.mult, ALU.add))
                own.link(V.tensor_scalar(t6, t6, MAGIC, None, ALU.add))
                own.link(V.tensor_scalar(t6, t6, -MAGIC, None, ALU.add))
                own.link(V.scalar_tensor_tensor(lg[:, r, :], t6, -TWO_PI_HI, lidt, ALU.mult, ALU.add))
                own.link(V.scalar_tensor_tensor(lg[:, r, :], t6, -TWO_PI_LO, lg[:, r, :], ALU.mult, ALU.add))
            own.link(V.tensor_scalar(lg[:, 8, :], lg[:, 8, :], float(np.pi / 2), None, ALU.add))
            V.tensor_scalar(lg[:, 7:9, :], lg[:, 7:9, :], 3.1415925, -3.1415925, ALU.min, ALU.max).then_inc(lam_dve, 1)
            dve.wait_ge(vec_pe, 1)
            V.tensor_copy(vec[:].rearrange("p v k -> p (v k)"), ps[:, 4, 0:56]).then_inc(vec_ready, 1)
            dve.wait_ge(vec_pe, 2)
            V.tensor_copy(nT[:], ps[:, 7, 0:32]).then_inc(vec_ready, 1)
            split_lo(dve, 0, 0)
            split_lo(dve, 1, 0)
            for k in range(KT + 1):
                if k < KT:
                    r = 2 * (k % 2)
                    dve.wait_ge(xt_done, k + 1)
                    V.tensor_copy(x[:, k, TS:N], ps[:, r, :])
                    V.tensor_copy(x[:, k, 0:TS], ps[:, r + 1, 0:TS]).then_inc(x_ready, 1)
                if k:
                    prep_lo(dve, k - 1, 0, V_MIX0)
            def scale_in(base, j, t):
                s = base % 2
                dve.wait_ge(slab_done, base + 1 + 2 * j)
                V.tensor_tensor(halves(tile(qkvo, t)), slab_ps(s), halves(R[:]), ALU.mult).then_inc(ps_free[s], 1)

            inv_rms(dve, 0)
            scale_in(0, 0, 24)
            split_lo(dve, 2, 0)
            scale_in(1, 0, 0)
            split_lo(dve, 3, 0)
            scale_in(2, 0, 1)
            split_lo(dve, 4, 0)
            dve.wait_ge(gate_pe, 1)
            dve.wait_ge(gate_in, 48)
            V.tensor_scalar(halves(gw[:, LI, :]), ps[0:8, 4:6, 0:HN], gs[:, BI:BI + 1], None, ALU.add)
            dve.wait_ge(gate_act, 1)
            own.link(V.tensor_scalar(halves(gw[:, LF, :]), ps[0:8, 6:8, 0:HN], gs[:, BF:BF + 1], 0.0, ALU.add, ALU.min))
            own.link(V.tensor_tensor(gw[:, LF, :], gw[:, LF, :], gw[:, GT1, :], ALU.subtract))
            dve.wait_ge(am_ready, 1)
            own.link(V.tensor_tensor_scan(gw[:, BC, :], gw[:, AM, :], gw[:, LF, :], 0.0, ALU.mult, ALU.add))
            first = slice(0, TS + 1, T)
            own.link(V.tensor_tensor(gw[:, GT2, 0:9], gw[:, LF, first], gs[:, M0:M0 + 9], ALU.add))
            own.link(V.tensor_copy(gw[:, GT1, :], gw[:, LI, :]))
            own.link(V.tensor_tensor(gw[:, GT1, first], gw[:, GT1, first], gw[:, GT2, 0:9], ALU.max))
            own.link(V.memset(gw[:, LF, first], -1e30))
            own.link(V.tensor_tensor_scan(gw[:, MM, :], gw[:, LF, :], gw[:, GT1, :], 0.0, ALU.add, ALU.max))
            u = qkvo[0:8, 24, :]
            dve.wait_ge(q4_clear, 1)
            V.tensor_copy(gs[:, MPT:MPT + B], gw[:, MM, T - 1:TS:T])
            V.tensor_copy(gs[:, MPT + B:MPT + B + 1], gw[:, MM, N - 1:N])
            own.link(V.tensor_tensor(u, gw[:, BC, :], gw[:, MM, :], ALU.subtract))
            own.link(V.tensor_tensor(Q4[0:8, :], gw[:, LI, :], gw[:, BC, :], ALU.subtract))
            own.link(V.tensor_tensor(gw[:, GT2, 0:TS].rearrange("h (b t) -> h b t", b=B),
                                     Q4[0:8, 0:TS].rearrange("h (b t) -> h b t", b=B),
                                     u[:, T - 1:TS:T].unsqueeze(2).to_broadcast([8, B, T]), ALU.add))
            own.link(V.tensor_scalar(gw[:, GT2, TS:N], Q4[0:8, TS:N], u[:, N - 1:N], None, ALU.add))
            V.tensor_copy(Q4[32:40, :], gw[:, GT2, :])
            V.tensor_scalar(Q4[64:72, :], gw[:, MM, :], -1.0, None, ALU.mult)
            own.link(V.tensor_tensor(gw[:, GT1, 0:TS].rearrange("h (b t) -> h b t", b=B),
                                     u[:, 0:TS].rearrange("h (b t) -> h b t", b=B),
                                     gs[:, M0:M0 + B].unsqueeze(2).to_broadcast([8, B, T]), ALU.add))
            V.tensor_tensor(gs[:, DEC:DEC + B], u[:, T - 1:TS:T], gs[:, M0:M0 + B], ALU.add).then_inc(m_ready, 1)
            V.tensor_copy(Q4[96:104, 0:TS], gw[:, GT1, 0:TS]).then_inc(q4_ready, 1)

            def pair_in(j):
                for q in range(2):
                    scale_in(3 + q, j, 2 + q + 2 * j)
                    split_lo(dve, 5 + q, j)

            def c_columns(ri):
                dve.wait_ge(craw_pe, ri + 1)
                for g2 in range(2):
                    hf = slice(g2 * SP, (g2 + 1) * SP)
                    last = V.tensor_copy(cT[hf, ri], ps[hf, 6:8, :].rearrange("p b (q g c) -> p (b q) g c", g=2, c=GC)[:, :, g2, :])
                last.then_inc(craw_ready, 1)

            pair_in(0)
            dve.wait_ge(lam_act, 3)
            sin, cos, a_re, a_im = (lg[:, n, :] for n in (10, 11, 12, 13))
            V.tensor_tensor(a_re, mag, cos, ALU.mult)
            V.tensor_tensor(t6, lr, lr, ALU.mult)
            V.tensor_tensor(t9, li, li, ALU.mult)
            own.link(V.tensor_tensor(a_im, mag, sin, ALU.mult))
            own.link(V.tensor_tensor(t6, t6, t9, ALU.add))
            own.link(V.reciprocal(lg[:, 5, :], t6))
            V.tensor_scalar(t19, a_re, -1.0, None, ALU.add)
            own.link(V.tensor_tensor(t9, a_im, li, ALU.mult))
            own.link(V.tensor_tensor(t6, t19, lr, ALU.mult))
            own.link(V.tensor_tensor(t6, t6, t9, ALU.add))
            own.link(V.tensor_tensor(lg[:, 14, :], t6, lg[:, 5, :], ALU.mult))
            V.tensor_tensor(t6, a_im, lr, ALU.mult)
            own.link(V.tensor_tensor(t9, t19, li, ALU.mult))
            own.link(V.tensor_tensor(t6, t6, t9, ALU.subtract))
            own.link(V.tensor_tensor(lg[:, 15, :], t6, lg[:, 5, :], ALU.mult))
            c, s = cos, sin
            for n in range(3):
                own.link(V.tensor_tensor(t6, c, c, ALU.mult))
                own.link(V.tensor_tensor(t9, s, s, ALU.mult))
                own.link(V.scalar_tensor_tensor(t19, c, 2.0, s, ALU.mult, ALU.mult))
                own.link(V.tensor_tensor(lg[:, 17, :], t6, t9, ALU.subtract))
                last = V.tensor_copy(lg[:, 18, :], t19)
                if n < 2:
                    own.link(last)
                c, s = lg[:, 17, :], lg[:, 18, :]
            last.then_inc(lam_dve, 1)
            pair_in(1)
            dve.wait_ge(lam_pe, 1)
            V.tensor_copy(s5s[:].rearrange("p v k -> p (v k)"), ps[:, 5, 0:224]).then_inc(craw_ready, 1)
            c_columns(0)
            pair_in(2)
            c_columns(1)
            with dve.Fori(3, 11) as j:
                pair_in(j)
            dve.wait_ge(gate_act, 2)
            dve.wait_ge(const_done, 2)
            V.tensor_tensor(gw[:, LF, 0:64].rearrange("k (h b) -> k h b", h=H),
                            ident[0:8, 0:8].unsqueeze(2).to_broadcast([8, H, B]),
                            gs[:, DEC:DEC + B].unsqueeze(1).to_broadcast([8, H, B]), ALU.mult).then_inc(dec_rhs, 1)
            for i in range(1, 12, 2):
                dve.wait_ge(kv_done, i + 1)
                r = 2 * (i % 4)
                if i < 4:
                    V.tensor_copy(Ktok[:, 1:5, i, :], ps[:, r, :].rearrange("p (i c) -> p i c", i=NB))
                    V.tensor_copy(Ktok[0:TS, 0, i, :], ps[0:TS, r + 1, 0:P]).then_inc(kv_dve, 1)
                else:
                    V.tensor_copy(Vtok[:, 1:5, i - 4, 0:DV], ps[:, r, :].rearrange("p (i c) -> p i c", i=NB))
                    V.tensor_copy(Vtok[0:TS, 0, i - 4, 0:DV], ps[0:TS, r + 1, 0:P]).then_inc(kv_dve, 1)
            dve.wait_ge(ex_ready, 2)
            dve.wait_ge(att_const, 1)
            own.link(V.memset(st5[:, 6, :], -0.5))

            def exponents(h):
                e = E[:, h % 2]
                dve.wait_ge(s_done, h + 1)
                if h >= 2:
                    dve.wait_ge(pv_done, h - 1)
                for j in range(NB):
                    w = L - j * P
                    V.tensor_scalar(e[:, OFF[j]:OFF[j] + w], ps[:, 0, j * P:L], TK[:, 1 + j, h:h + 1], 0.0, ALU.add, ALU.min)
                V.tensor_scalar(e[0:TS, 1280:1344], ps[0:TS, 3, 320:384], TK[0:TS, 0, h:h + 1], 0.0,
                                ALU.add, ALU.min).then_inc(arg_done, 1)

            def weights(h):
                e = E[:, h % 2]
                dve.wait_ge(exp_done, h + 1)
                flat = ps[:].rearrange("p b c -> p (b c)")
                V.scalar_tensor_tensor(e[:, 0:1280], flat[:, 512:1792], DK ** -0.5, e[:, 0:1280], ALU.mult, ALU.mult)
                V.scalar_tensor_tensor(e[0:TS, 1280:1344], flat[0:TS, 1792:1856], DK ** -0.5, e[0:TS, 1280:1344],
                                       ALU.mult, ALU.mult).then_inc(p_done, 1)

            def sample_queries(h):
                hp = h % 2 * DK
                for b2 in range(2):
                    last = V.tensor_copy(
                        Qblk[b2 * DK:(b2 + 1) * DK, :].rearrange("p (b c) -> p b c", b=4)[:, :, b2 * T:(b2 + 1) * T],
                        qkvo[hp:hp + DK, h // 2, 0:TS].rearrange("p (b a t) -> p b a t", a=2, t=T)[:, :, b2, :])
                last.then_inc(qblk_ready, 1)

            def keys(h):
                s = h % 2
                if h >= 2:
                    dve.wait_ge(upb_done, h - 1)
                kc = slice(h % 2 * DK, (h % 2 + 1) * DK)
                own.link(V.tensor_scalar(Kws[0:TS, s, 0, :], Ktok[0:TS, 0, h // 2, kc], EX[0:TS, 0, h:h + 1], DK ** -0.5,
                                         ALU.mult, ALU.mult))
                V.scalar_tensor_tensor(Kws[:, s, 1:5, :], Ktok[:, 1:5, h // 2, kc], DK ** -0.5,
                                       EX[:, 1:5, h:h + 1].to_broadcast([P, NB, DK]), ALU.mult, ALU.mult)
                V.tensor_tensor(Kblk[:, s], Kws[0:TS, s, 0, :].unsqueeze(1).to_broadcast([TS, B, DK]),
                                MB[:].unsqueeze(2).to_broadcast([TS, B, DK]), ALU.mult).then_inc(kws_ready, 1)

            def decayed(h, b4, new):
                c = Cst[:, h % 2, b4, :]
                return V.scalar_tensor_tensor(c, c, dcy[:, h, b4:b4 + 1], new, ALU.mult, ALU.add)

            def states_a(h):
                dve.wait_ge(upa_done, h + 1)
                for b4 in range(3):
                    last = decayed(h, b4, ps[:, 7, b4 * E1:(b4 + 1) * E1])
                last.then_inc(ca_done, 1)

            def states_b(h):
                dve.wait_ge(upb_done, h + 1)
                if h >= 2:
                    dve.wait_ge(c_out[h % 2], 16 * 3 * (h // 2))
                V.tensor_copy(CP[:, h % 2, :], ps[0:DK, 4, E1:E1 + DV])
                V.tensor_copy(nP[:, h:h + 1], ps[0:DK, 4, E1 + DV:2 * E1])
                own.link(decayed(h, 3, ps[:, 4, 0:E1]))
                dve.wait_ge(ca_done, h + 1)
                V.tensor_copy(nN[:, :, h], Cst[:, h % 2, :, DV]).then_inc(c_new, 1)

            def gated(h):
                dve.wait_ge(osig_ready, h + 1)
                dve.wait_ge(ht_done, h + 1)
                o = qkvo[:, 16 + h]
                V.scalar_tensor_tensor(o[:, TS:N], ps[:, 6, :], gain(V_HEAD, h), o[:, TS:N], ALU.mult, ALU.mult)
                V.scalar_tensor_tensor(o[:, 0:TS], ps[:, 7, 448:512], gain(V_HEAD, h), o[:, 0:TS], ALU.mult,
                                       ALU.mult).then_inc(hf_ready, 1)

            def gated_lo(h):
                dve.wait_ge(hhi_done, h + 1)
                V.tensor_tensor(hid_lo[:, h], qkvo[:, 16 + h], hid_hi[:, h].bitcast(F32), ALU.subtract).then_inc(hid_ready, 1)

            keys(0)
            sample_queries(0)
            exponents(0)
            weights(0)
            for h in range(H):
                if h + 1 < H:
                    exponents(h + 1)
                if h:
                    states_b(h - 1)
                    gated(h - 1)
                if h + 1 < H:
                    weights(h + 1)
                    keys(h + 1)
                if h:
                    gated_lo(h - 1)
                dve.wait_ge(ot_act, h + 1)
                V.tensor_tensor(OT[0:TS, 0, :], ps[0:TS, 5, E1:2 * E1], Is[:], ALU.add).then_inc(ot_ready, 1)
                if h + 1 < H:
                    sample_queries(h + 1)
                dve.wait_ge(ot_ready, h + 1)
                own.link(V.scalar_tensor_tensor(st5[:, 0, :], OT[:, :, DV], -1.0, OT[:, :, DV], ALU.mult, ALU.max))
                own.link(V.tensor_tensor(st5[:, 0, :], st5[:, 0, :], EX[:, :, 32 + h], ALU.max))
                own.link(V.reciprocal(st5[:, 1, :], st5[:, 0, :]))
                own.link(V.tensor_tensor(st5[:, 3, :], st5[:, 1, :], st5[:, 1, :], ALU.mult))
                dve.wait_ge(ssq_done, h + 1)
                own.link(V.tensor_tensor(st5[:, 3, :], st5[:, 3, :], st5[:, 2, :], ALU.mult))
                V.tensor_scalar(st5[:, 4, :], st5[:, 3, :], 1.0 / DV, EPS, ALU.mult, ALU.add).then_inc(ms_ready, 1)
                states_a(h)
                dve.wait_ge(rstd_ready, h + 1)
                own.link(V.tensor_tensor(st5[:, 7, :], st5[:, 5, :], st5[:, 1, :], ALU.mult))
                V.tensor_tensor(Htok[:], OT[:, :, 0:DV], st5[:, 7, :].unsqueeze(2).to_broadcast([P, 5, DV]),
                                ALU.mult).then_inc(htok_ready, 1)
            states_b(H - 1)
            gated(H - 1)
            gated_lo(H - 1)

            def add_down(base, j, m):
                s = base % 2
                dve.wait_ge(slab_done, base + 1 + 2 * j)
                V.tensor_tensor(halves(tile(x, m)), halves(tile(x, m)), slab_ps(s), ALU.add).then_inc(ps_free[s], 1)

            with dve.Fori(0, 4) as j:
                for q in range(2):
                    add_down(25 + q, j, 2 * j + q)
                    prep_lo(dve, 2 * j + q, 1, V_FFN0)
                    split_lo(dve, 27 + q, j)

            steps = lambda ap: ap.rearrange("p (t b) -> p b t", t=T)
            blocks = lambda ap: ap.rearrange("p (b t) -> p b t", t=T)

            def ffn_dve(l):
                up, down = I_FFN[l], I_FFN[l] + 8
                inv_rms(dve, 1 + 2 * l)

                def tile_up(base, j, e, k):
                    s = base % 2
                    dve.wait_ge(ps_free[s], base // 2 + 1 + j)
                    V.tensor_tensor(tbuf[:], rbuf[:], R[:], ALU.mult).then_inc(scaled, 1)
                    split_lo(dve, base + 2, j)
                    dve.wait_ge(hhi_done, HID0[l] + 1 + e)
                    V.tensor_tensor(tile(hid_lo, k), qbuf[:], tile(hid_hi, k).bitcast(F32),
                                    ALU.subtract).then_inc(hid_ready, 1)

                with dve.Fori(0, 4) as j:
                    for q in range(2):
                        tile_up(up + q, j, q + 2 * j, q + 2 * j)
                with dve.Fori(0, FF - 1) as f:
                    with dve.Fori(0, 4) as j:
                        for q in range(2):
                            add_down(down + q, 8 * f + j, 2 * j + q)
                            split_lo(dve, down + 2 + q, 8 * f + j)
                    with dve.Fori(0, 4) as j:
                        for q in range(2):
                            tile_up(up + 16 + q, 8 * f + j, 8 + q + 8 * f + 2 * j, q + 2 * j)
                if l == 0:
                    for k in range(KT):
                        add_down(down + 48 + k, 0, k)
                        wait_x(dve, 2, k)
                        if k == 0:
                            dve.wait_ge(slab_done, down + 48)
                        V.tensor_scalar(steps(unat[:, k]), blocks(x[:, k]), gain(V_MIX1, k), None, ALU.mult).then_inc(u_ready, 1)
                        split_lo(dve, down + 50 + k, 0)
                    return
                with dve.Fori(0, 3) as j:
                    for q in range(2):
                        add_down(down + 48 + q, j, 2 * j + q)
                        split_lo(dve, down + 50 + q, j)
                for q in range(2):
                    add_down(down + 54 + q, 0, 6 + q)

            ffn_dve(0)
            dve.wait_ge(r2_act, 1)
            V.reciprocal(R2[:], R2[:]).then_inc(r2_ready, 1)
            dve.wait_ge(r2_ready, 1)

            def normalised(k):
                dve.wait_ge(u2_in[k // 4], 16 * T)
                u = U2[:, 8 * k:8 * k + 8, :]
                V.tensor_tensor(u, u, R2[:].unsqueeze(1).to_broadcast([P, 8, COLS]), ALU.mult).then_inc(un_ready, 1)

            normalised(0)
            normalised(1)

            def states(k):
                g, s = slice(4 * k, 4 * k + 4), k % 2
                c, sn = EC[:, g], ES[:, g]
                vr, vi = (ps[:, 4 + ri, 0:4 * COLS].rearrange("p (q c) -> p q c", q=4)[:, :, B:COLS] for ri in range(2))
                v0 = ps[:, 4:6, 0:4 * COLS].rearrange("p r (q c) -> p r q c", q=4)[:, :, :, 0:B]
                V.tensor_copy(rho[:, :, 1:SP], s5s[:, MAG8, g].unsqueeze(2).to_broadcast([P, 4, SP - 1]))
                dve.wait_ge(v_done, k + 1)
                V.tensor_tensor(rot[:, 0], vr, c, ALU.mult)
                V.tensor_tensor(rot[:, 1], vi, sn, ALU.mult)
                V.tensor_tensor(rot[:, 2], vi, c, ALU.mult)
                V.tensor_tensor(rot[:, 3], vr, sn, ALU.mult)
                if k == 0:
                    dve.wait_ge(u_out, 16 * KT)
                own.link(V.tensor_copy(hN[:, :, :, g].rearrange("p r b g -> p r g b"), v0))
                V.tensor_tensor(rot[:, 0], rot[:, 0], rot[:, 1], ALU.add)
                V.tensor_tensor(rot[:, 2], rot[:, 2], rot[:, 3], ALU.subtract).then_inc(h_ready, 1)
                dve.wait_ge(h_ready, k + 1)
                flat = lambda ap: ap.rearrange("p q c -> p (q c)")
                V.tensor_tensor_scan(flat(rot[:, 1]), flat(rho[:]), flat(rot[:, 0]), 0.0, ALU.mult, ALU.add)
                own.link(V.tensor_tensor_scan(flat(rot[:, 3]), flat(rho[:]), flat(rot[:, 2]), 0.0, ALU.mult, ALU.add))
                V.tensor_tensor(rot[:, 0], rot[:, 1], c, ALU.mult)
                V.tensor_tensor(rot[:, 2], rot[:, 3], sn, ALU.mult)
                V.tensor_tensor(rot[:, 1], rot[:, 1], sn, ALU.mult)
                own.link(V.tensor_tensor(rot[:, 3], rot[:, 3], c, ALU.mult))
                if k >= 2:
                    dve.wait_ge(sy_done, k - 1)
                V.tensor_tensor(Hst[:, s, 0, :, B + 1:], rot[:, 0], rot[:, 2], ALU.subtract)
                V.tensor_tensor(Hst[:, s, 1, :, B + 1:], rot[:, 1], rot[:, 3], ALU.add)
                own.link(V.tensor_copy(Hst[:, s, :, :, 0:B], h0[:, :, :, g].rearrange("p r b g -> p r g b")))
                V.tensor_copy(hP[:, :, g], Hst[:, s, :, :, COLS]).then_inc(hst_ready, 1)

            def skip(k):
                if k:
                    dve.wait_ge(hid_ready, HID0[1] - KT + k)
                own.link(V.scalar_tensor_tensor(yv[:], x[:, k], gain(V_MIX1, k), R[:], ALU.mult, ALU.mult))
                dve.wait_ge(yn_in, 16 * (k + 1))
                V.scalar_tensor_tensor(blocks(yv[:]), blocks(yv[:]), gain(V_SKIP, k), steps(yn[:]), ALU.mult, ALU.add).then_inc(dskip, 1)
                dve.wait_ge(hhi_done, 41 + k)
                V.tensor_tensor(hid_lo[:, k], yv[:], hid_hi[:, k].bitcast(F32), ALU.subtract).then_inc(hid_ready, 1)

            dve.wait_ge(s5_set, 1)
            for i in range(KT + 3):
                if i < KT:
                    states(i)
                if i + 2 < KT:
                    normalised(i + 2)
                if i == 0:
                    inv_rms(dve, 2)
                if i >= 3:
                    skip(i - 3)
            with dve.Fori(0, 4) as j:
                for q in range(2):
                    base = I_GLU + 2 * q
                    dve.wait_ge(ps_free[1], base // 2 + 1 + 2 * j)
                    V.tensor_scalar(sbuf[:], gbuf[:], 1.0, 0.5, ALU.add, ALU.mult).then_inc(sig_done, 1)
                    split_lo(dve, base + 2, 2 * j)
                    split_lo(dve, base + 3, 2 * j)
                    dve.wait_ge(sig_done, 1 + q + 2 * j)
                    dve.wait_ge(slab_done, base + 2 + 4 * j)
                    V.tensor_tensor(halves(tb2[:]), slab_ps(0), halves(sbuf[:]), ALU.mult).then_inc(glu_done, 1)
                    dve.wait_ge(glu_done, 1 + q + 2 * j)
                    k = q + 2 * j
                    V.tensor_tensor(tile(x, k), tile(x, k), tb2[:], ALU.add).then_inc(ps_free[0], 1)
                    prep_lo(dve, k, 2, V_FFN1)
            ffn_dve(1)
            dve.wait_ge(fin_act, 1)
            V.reciprocal(fin[0:TS, 0:1], fin[0:TS, 0:1])
            V.reciprocal(fin[:, 1:5], fin[:, 1:5]).then_inc(fin_ready, 1)
            dve.wait_ge(fin_ready, 1)
            for i in range(5):
                n = TS if i == 0 else P
                dve.wait_ge(yt_done, i + 1)
                if i >= 2:
                    dve.wait_ge(y_out[i % 2], 16 * (i // 2))
                V.tensor_scalar(ybuf[0:n, i % 2, 512:1024], ps[0:n, YB[i] + 1, :], fin[0:n, i:i + 1], None, ALU.mult).then_inc(y_dve, 1)

        @block.tensor
        def _(pe):
            pe.wait_ge(const_done, 1)
            pe.wait_ge(vec_in, 16 * 5)
            nc.tensor.transpose(ps[:, 4, 0:56], vrow[:], ident[0:56, 0:56]).then_inc(vec_pe, 1)
            pe.wait_ge(nrow_in, 16 * 8)
            nc.tensor.transpose(ps[:, 7, 0:32], nrow[:], ident[0:32, 0:32]).then_inc(vec_pe, 1)
            pe.wait_ge(x_in, 16 * 5)
            for k in range(KT):
                r = 2 * (k % 2)
                if k >= 2:
                    pe.wait_ge(x_ready, k - 1)
                for i in range(NB):
                    nc.tensor.transpose(ps[:, r, i * P:(i + 1) * P], xtok[:, 1 + i, k * P:(k + 1) * P], ident[:])
                nc.tensor.transpose(ps[:, r + 1, 0:TS], xtok[0:TS, 0, k * P:(k + 1) * P],
                                    ident[0:TS, 0:TS]).then_inc(xt_done, 1)
            pe.wait_ge(x_ready, KT)
            pe.wait_ge(const_done, 2)
            xg, hid = (xg_hi, xg_lo), (hid_hi, hid_lo)
            product(pe, 0, 0, xg, (xg_ready, 0))
            pe.wait_ge(vec_ready, 1)
            stats(pe, 0)
            product(pe, 1, 0, xg)
            product(pe, 2, 0, xg)
            pe.wait_ge(vec_ready, 2)
            pe.wait_ge(R_ready, 1)
            for g in range(2):
                for c in range(2):
                    last = nc.tensor.matmul(ps[0:8, 4 + 2 * g + c, 0:HN], ident[:, GATE_ROW + 8 * g:GATE_ROW + 8 * g + 8],
                                            qkvo[:, 24, c * HN:(c + 1) * HN], start=True, stop=True)
            last.then_inc(gate_pe, 1)

            def pair_in(j):
                for q in range(2):
                    product(pe, 3 + q, j, xg)

            def c_turn(ri):
                for k in range(KT):
                    last = nc.tensor.transpose(ps[:, 6 + k // 4, k % 4 * P:(k % 4 + 1) * P],
                                               craw[:, ri, k].rearrange("p a b -> p (a b)"), ident[:])
                last.then_inc(craw_pe, 1)

            pair_in(0)
            pair_in(1)
            pe.wait_ge(lam_dve, 3)
            pe.wait_ge(gate_act, 1)
            pe.wait_ge(m_ready, 1)
            for v in range(7):
                last = nc.tensor.transpose(ps[:, 5, v * GP:(v + 1) * GP], lg[:, 12 + v, :], ident[0:GP, 0:GP])
            last.then_inc(lam_pe, 1)
            pe.wait_ge(craw_in, 64)
            c_turn(0)
            pair_in(2)
            pe.wait_ge(craw_ready, 2)
            c_turn(1)
            with pe.Fori(3, 11) as j:
                pair_in(j)
            pe.wait_ge(q4_ready, 1)
            pe.wait_ge(craw_ready, 3)
            nc.tensor.transpose(ps[0:TS, 4, 0:P], Q4[:, 0:TS], ident[:])
            for i in range(NB):
                nc.tensor.transpose(ps[:, 5, i * P:(i + 1) * P], Q4[:, TS + i * P:TS + (i + 1) * P], ident[:])
            pe.wait_ge(dec_rhs, 1)
            nc.tensor.matmul(ps[:, 6, 0:64], ones[0:8, :], gw[:, LF, 0:64], start=True, stop=True).then_inc(tk_pe, 1)
            pe.wait_ge(ps_free[0], 13)
            pe.wait_ge(ps_free[1], 12)
            pe.wait_ge(ex_ready, 2)
            for i in range(12):
                r = 2 * (i % 4)
                if i >= 4:
                    if i % 2:
                        pe.wait_ge(kv_dve, i // 2 - 1)
                    else:
                        pe.wait_ge(kv_act, i // 2 - 1)
                for n in range(NB):
                    nc.tensor.transpose(ps[:, r, n * P:(n + 1) * P], qkvo[:, 4 + i, TS + n * P:TS + (n + 1) * P], ident[:])
                nc.tensor.transpose(ps[0:TS, r + 1, 0:P], qkvo[:, 4 + i, 0:TS], ident[:]).then_inc(kv_done, 1)
            pe.wait_ge(kv_act, 6)
            pe.wait_ge(kv_dve, 6)
            pe.wait_ge(att_const, 2)

            def scores(h):
                if h:
                    pe.wait_ge(p_done, h)
                hp = h % 2 * DK
                q, k = qkvo[hp:hp + DK, h // 2], qkvo[hp:hp + DK, 4 + h // 2]
                u = qkvo[0:8, 24]
                nc.tensor.matmul(ps[:, 0, :], SEL[:, h, :], u[:, TS:N], start=True, stop=True)
                for j, (b, c) in enumerate(((1, 0), (2, 0), (3, 0), (2, 384))):
                    w = L - j * P
                    nc.tensor.matmul(ps[:, b, c:c + w], k[:, TS + j * P:TS + (j + 1) * P], q[:, TS + j * P:N],
                                     start=True, stop=True)
                nc.tensor.matmul(ps[0:TS, 3, 256:320], k[:, 0:TS], q[:, 0:TS], start=True, stop=True)
                nc.tensor.matmul(ps[0:TS, 3, 320:384], SEL[:, h, 0:TS], u[:, 0:TS], start=True, stop=True).then_inc(s_done, 1)

            def heads_out(h):
                pe.wait_ge(htok_ready, h + 1)
                pe.wait_ge(ca_done, h + 1)
                if h:
                    pe.wait_ge(hf_ready, h)
                for i in range(NB):
                    nc.tensor.transpose(ps[:, 6, i * P:(i + 1) * P], Htok[:, 1 + i, :], ident[:])
                nc.tensor.transpose(ps[:, 7, 448:512], Htok[0:TS, 0, :], ident[0:TS, 0:TS]).then_inc(ht_done, 1)

            def sums(h):
                e = E[:, h % 2]
                pe.wait_ge(p_masked, h + 1)
                pe.wait_ge(qblk_ready, h + 1)
                pe.wait_ge(ncol_ready, h + 1)
                if h:
                    pe.wait_ge(ot_ready, h)
                    pe.wait_ge(c_new, h)
                for i in range(NB):
                    o = ps[:, 4, i * E1:(i + 1) * E1] if i < 3 else ps[:, 5, 0:E1]
                    for j in range(i + 1):
                        c = OFF[j] + (i - j) * P
                        nc.tensor.matmul(o, e[:, c:c + P], Vtok[:, 1 + j, h, :], start=(j == 0), stop=(j == i))
                nc.tensor.matmul(ps[0:TS, 5, E1:2 * E1], e[0:TS, 1280:1344], Vtok[0:TS, 0, h, :], start=True, stop=True)
                for b4 in range(4):
                    last = nc.tensor.matmul(ps[0:TS, 5, 2 * E1:3 * E1], Qblk[:, b4 * TS:(b4 + 1) * TS], Cst[:, h % 2, b4, :],
                                            start=(b4 == 0), stop=(b4 == 3))
                last.then_inc(pv_done, 1)

            def key_values(h, b4, out):
                return nc.tensor.matmul(out, Kblk[:, h % 2, 2 * b4:2 * b4 + 2, :].rearrange("s b d -> s (b d)"),
                                        Vtok[0:TS, 0, h, :], start=True, stop=True)

            def updates_a(h):
                pe.wait_ge(kws_ready, h + 1)
                if h:
                    pe.wait_ge(hf_ready, h)
                for b4 in range(3):
                    last = key_values(h, b4, ps[:, 7, b4 * E1:(b4 + 1) * E1])
                last.then_inc(upa_done, 1)

            def updates_b(h):
                pe.wait_ge(ot_ready, h + 1)
                key_values(h, 3, ps[:, 4, 0:E1])
                for j in range(NB):
                    last = nc.tensor.matmul(ps[0:DK, 4, E1:2 * E1], Kws[:, h % 2, 1 + j, :], Vtok[:, 1 + j, h, :],
                                            start=(j == 0), stop=(j == NB - 1))
                last.then_inc(upb_done, 1)

            scores(0)
            for h in range(H):
                if h + 1 < H:
                    scores(h + 1)
                if h:
                    updates_b(h - 1)
                    heads_out(h - 1)
                sums(h)
                updates_a(h)
            updates_b(H - 1)
            heads_out(H - 1)
            pe.wait_ge(c_new, H)
            pe.wait_ge(hf_ready, H)
            nc.tensor.transpose(ps[0:32, 6, 256:384], nN[:].rearrange("p b h -> p (b h)"), ident[:])
            nc.tensor.transpose(ps[0:H, 7, 0:DK], nP[:], ident[0:DK, 0:DK]).then_inc(n_pe, 1)
            product(pe, 25, 0, hid, (hid_ready, 0))
            product(pe, 26, 0, hid)
            with pe.Fori(0, 3) as j:
                for q in range(2):
                    product(pe, 27 + q, j, hid)

            def taps():
                pe.wait_ge(bb_done, 1)
                for k in range(KT):
                    for q in range(4):
                        g = 4 * k + q
                        for ri in range(2):
                            last = nc.tensor.matmul(ps[32 * q:32 * q + 32, 6 + k // 4, k % 4 * P:(k % 4 + 1) * P],
                                                    bblk[:, ri, g].rearrange("p a c -> p (a c)"),
                                                    CA[:, ri, g, 0:T, :].rearrange("p j c -> p (j c)"),
                                                    start=(ri == 0), stop=(ri == 1))
                pe.wait_ge(st5_in, 64)
                for i in range(4):
                    last = nc.tensor.transpose(ps[:, 4, i * P:(i + 1) * P], srow[:, i, :], ident[:])
                last.then_inc(taps_done, 1)

            def ffn_pe(l):
                up, down = I_FFN[l], I_FFN[l] + 8
                product(pe, up, 0, xg, (xg_ready, KT * (1 + l)))
                stats(pe, 1 + 2 * l)
                product(pe, up + 1, 0, xg)
                with pe.Fori(0, 3) as j:
                    for q in range(2):
                        product(pe, up + 2 + q, j, xg)
                with pe.Fori(0, FF - 1) as f:
                    product(pe, down, 8 * f, hid, (hid_ready, HID0[l] + 8 * f))
                    product(pe, down + 1, 8 * f, hid)
                    with pe.Fori(0, 3) as j:
                        for q in range(2):
                            product(pe, down + 2 + q, 8 * f + j, hid)
                    with pe.Fori(0, 4) as j:
                        for q in range(2):
                            product(pe, up + 16 + q, 8 * f + j, xg)
                product(pe, down + 48, 0, hid, (hid_ready, HID0[l] + 24))
                for i in range(1, KT):
                    if l == 0 and i == 3:
                        taps()
                    product(pe, down + 48 + i, 0, hid)

            ffn_pe(0)

            def gains_turn(k):
                pe.wait_ge(gs_ready, k + 1)
                if k >= 2:
                    pe.wait_ge(gt_ready, k - 1)
                for ri in range(2):
                    for q in range(4):
                        last = nc.tensor.transpose(ps[:, 2 * (k % 2) + ri, q * P:(q + 1) * P], GS[:, ri, q, :], ident[:])
                last.then_inc(gt_done, 1)

            def block_sums(k):
                s = k % 2
                pe.wait_ge(gt_ready, k + 1)
                if k:
                    pe.wait_ge(h_ready, k)
                pe.wait_ge(un_ready, k + 1)
                for q in range(4):
                    for g2 in range(2):
                        hf = slice(g2 * SP, (g2 + 1) * SP)
                        for ri in range(2):
                            last = nc.tensor.matmul(ps[hf, 4 + ri, q * COLS:(q + 1) * COLS], GT[:, s, 4 * ri + q, hf],
                                                    U2[:, 8 * k + 2 * q + g2, :], start=True, stop=True)
                last.then_inc(v_done, 1)

            def answers(k):
                s = k % 2
                pe.wait_ge(hst_ready, k + 1)
                pe.wait_ge(mt_in[s], 16 * T * (k // 2 + 1))
                if k:
                    pe.wait_ge(yev_ready, k)
                for q in range(4):
                    for g2 in range(2):
                        g8, st = 2 * q + g2, slice(g2 * SP, (g2 + 1) * SP)
                        for hf in range(2):
                            o = ps[hf * 64:(hf + 1) * 64, 6 + g2, q * COLS:(q + 1) * COLS]
                            nc.tensor.matmul(o, MT[:, s, g8, hf * 64:(hf + 1) * 64], U2[:, 8 * k + g8, :], start=True, stop=False)
                            for ri in range(2):
                                last = nc.tensor.matmul(
                                    o, CA[st, ri, 4 * k + q, 1 + 4 * hf:5 + 4 * hf, :].rearrange("p j c -> p (j c)"),
                                    Hst[st, s, ri, q, 0:COLS], start=False, stop=(ri == 1))
                last.then_inc(sy_done, 1)

            pe.wait_ge(ps_free[0], I_GLU // 2 + 1)
            pe.wait_ge(ps_free[1], I_GLU // 2)
            gains_turn(0)
            pe.wait_ge(acc_done, 3 * KT)
            pe.wait_ge(row_sel, 1)
            pe.wait_ge(kt_act, 2)
            for i in range(T):
                hf, c = slice(i // 4 * 64, i // 4 * 64 + 64), (7 - i % 4) * GC
                last = nc.tensor.matmul(ps[hf, 6, 0:COLS], rowsel[:, c:c + 64], acc[:, T - 1 - i::T],
                                        start=(i % 4 == 0), stop=(i % 4 == 3))
            last.then_inc(r2_pe, 1)
            pe.wait_ge(h0_act, 1)
            stats(pe, 2)
            gains_turn(1)
            pe.wait_ge(rms_done, 3)
            pe.wait_ge(r2_act, 1)
            for i in range(KT + 1):
                if 0 < i < KT - 1:
                    gains_turn(i + 1)
                if i < KT:
                    block_sums(i)
                if i:
                    answers(i - 1)
            pe.wait_ge(pool_pre, 1)
            for i in range(4):
                nc.tensor.transpose(ps[:, 4, i * P:(i + 1) * P], hN[:, i // 2].rearrange("p b g -> p (b g)")[:, i % 2 * P:(i % 2 + 1) * P], ident[:])
            nc.tensor.transpose(ps[0:2 * GP, 5, 0:P], hP[:].rearrange("p r g -> p (r g)"), ident[:]).then_inc(ssend_pe, 1)
            product(pe, I_GLU, 0, hid, (hid_ready, 40))
            product(pe, I_GLU + 1, 0, hid)
            with pe.Fori(0, 7) as j:
                for q in range(2):
                    product(pe, I_GLU + 2 + q, j, hid)
            pe.wait_ge(ssend_rows, 1)
            ffn_pe(1)
            pe.wait_ge(acc_done, 5 * KT)
            nc.tensor.matmul(ps[0:TS, 4, 0:2], acc[:, 0:TS], ones[:, 0:2], start=True, stop=True)
            for i in range(NB):
                last = nc.tensor.matmul(ps[:, 4, 2 + 2 * i:4 + 2 * i], acc[:, TS + i * P:TS + (i + 1) * P], ones[:, 0:2],
                                        start=True, stop=True)
            last.then_inc(fin_pe, 1)
            pe.wait_ge(xf_ready, KT)
            pe.wait_ge(ps_free[0], N_SLABS // 2 + 1)
            pe.wait_ge(ps_free[1], N_SLABS // 2)
            for i in range(5):
                cols = slice(0, TS) if i == 0 else slice(TS + (i - 1) * P, TS + i * P)
                n = cols.stop - cols.start
                if i >= 3:
                    pe.wait_ge(y_act, i - 2)
                    pe.wait_ge(y_dve, i - 2)
                for k in range(KT):
                    last = nc.tensor.transpose(ps[0:n, YB[i] + k // 4, k % 4 * P:(k % 4 + 1) * P], xf[:, k, cols], ident[:])
                last.then_inc(yt_done, 1)


_INS = ['x_prompt', 'x_sample', 'state_mlstm_C', 'state_mlstm_n', 'state_mlstm_m', 'state_s5_re', 'state_s5_im',
        'norm_mix_g', 'norm_ffn_g', 'norm_final_g', 'mlstm_w_in', 'mlstm_b_i', 'mlstm_b_f', 'mlstm_head_norm_g',
        'mlstm_w_out', 's5_lambda_re', 's5_lambda_im', 's5_log_dt', 's5_b_re', 's5_b_im', 's5_c_re', 's5_c_im',
        's5_d', 's5_w_glu', 'ffn_w_up', 'ffn_w_down']
_OUTS = [(1, L, D), (B, T, D), (1, 1, H, DK, DV), (1, 1, H, DK), (1, 1, H), (1, 1, G, SP), (1, 1, G, SP),
         (1, B, H, DK, DV), (1, B, H, DK), (1, B, H), (1, B, G, SP), (1, B, G, SP)]


def kernel(**inputs):
    import concourse.bacc as _bacc
    from concourse.bass_utils import run_bass_kernel_spmd as _run

    nc = _bacc.Bacc("TRN2", target_bir_lowering=False, num_devices=1)
    arrays, args = {}, []
    for name in _INS:
        a = np.ascontiguousarray(inputs[name])
        arrays[f"in_{name}"] = a
        args.append(nc.dram_tensor(f"in_{name}", a.shape, mybir.dt.from_np(a.dtype), kind="ExternalInput").ap())
    for i, shape in enumerate(_OUTS):
        args.append(nc.dram_tensor(f"out_{i}", shape, F32, kind="ExternalOutput").ap())
    build(nc, *args)
    r = _run(nc, [arrays], core_ids=[0])
    return tuple(r.results[0][f"out_{i}"] for i in range(len(_OUTS)))
```

```python
from contextlib import ExitStack

import numpy as np

import concourse.bass as bass
from concourse import mybir

ALU = mybir.AluOpType
ACT = mybir.ActivationFunctionType
F32 = mybir.dt.float32
F32R = mybir.dt.float32r

P = 128
D = 1024
KT = D // P
B = 8
T = 8
TS = B * T
L = 512
N = TS + L
HN = N // 2
COLS = N // T
NB = L // P
H = 8
DK = 64
DV = 128
E1 = DV + 1
GATE_ROW = 96 + 16
FF = 4
G = 64
GC = 16
SP = 64
GP = G // 2
EPS = 1e-6
PAD = (T - 1) * GC
TAPS = PAD + T * GC
TWO_PI_HI = 6.28125
TWO_PI_LO = 0.0019353071795864769
MAGIC = 12582912.0

I_QKVO = 1
I_OUT = 25
I_FFN = (33, 113)
I_GLU = 97
HID0 = (8, 48)
N_SLABS = 177
V_MIX0, V_MIX1, V_FFN0, V_FFN1, V_FIN, V_HEAD, V_SKIP = range(7)


def build(nc, x_prompt, x_sample, st_C, st_n, st_m, st_re, st_im, g_mix, g_ffn, g_fin, w_in, b_i, b_f,
          g_head, w_out, lam_re, lam_im, log_dt, b_re, b_im, c_re, c_im, s5_d, w_glu, w_up, w_down,
          y_prompt, y_sample, p_C, p_n, p_m, p_re, p_im, s_C, s_n, s_m, s_re, s_im):
    d_taps = nc.dram_tensor("d_taps", (D, TAPS), F32, kind="Internal").ap()
    d_u = nc.dram_tensor("d_u", (D, T, COLS), F32, kind="Internal").ap()
    d_y = nc.dram_tensor("d_y", (D, T, COLS), F32, kind="Internal").ap()

    slab_in = w_in[0].rearrange("(k p) c -> p k c", p=P)
    slab_out = w_out[0].rearrange("(k p) c -> p k c", p=P)
    slab_glu = w_glu[0].rearrange("(k p) c -> p k c", p=P)
    slab_up = [w_up[l].rearrange("(k p) c -> p k c", p=P) for l in range(2)]
    slab_down = [w_down[l].rearrange("(f k p) c -> p f k c", p=P, k=KT) for l in range(2)]

    ctx = ExitStack()
    with ctx:
        def sb(name, shape, dt=F32, stack=None):
            return (stack or ctx).enter_context(nc.sbuf_tensor(name, shape, dt))

        x = sb("x", [P, KT, N])
        raw = sb("raw", [P, 2, KT, P])
        whi = sb("whi", [P, 2, KT, P], F32R)
        wlo = sb("wlo", [P, 2, KT, P], F32R)
        R = sb("R", [P, N])
        acc = sb("acc", [P, N])
        sqb = sb("sqb", [P, N])
        ident = sb("ident", [P, P])
        ones = sb("ones", [P, P])
        vec = sb("vec", [P, 7, KT])
        eps = sb("eps", [P, 1])
        s5s = sb("s5s", [P, 7, GP])
        cT = sb("cT", [P, 2, GP, GC])
        nT = sb("nT", [P, 32])
        nN = sb("nN", [P, 4, H])
        nP = sb("nP", [DK, H])
        dcy = sb("dcy", [P, H, 4])
        gs = sb("gs", [8, 32])
        fin = sb("fin", [P, 8])
        A_RE, A_IM, CF_RE, CF_IM, MAG8, COS8, SIN8 = range(7)
        M0, BI, BF, DEC, MPT = 0, 9, 10, 11, 20

        with ExitStack() as early:
            xtok = sb("xtok", [P, 5, D], stack=early)
            gw = sb("gw", [8, 7, N], stack=early)
        with ExitStack() as late_taps:
            late = sb("late", [P, 2, KT, N], stack=late_taps)
        Q4 = xtok[:, 0, 0:N]
        LF, LI, AM, BC, MM, GT1, GT2 = range(7)
        hid_hi = sb("hid_hi", [P, KT, N], F32R)
        hid_lo = sb("hid_lo", [P, KT, N], F32R)

        xg_stack = ExitStack()
        xg_hi = sb("xg_hi", [P, KT, N], F32R, stack=xg_stack)
        xg_lo = sb("xg_lo", [P, KT, N], F32R, stack=xg_stack)
        with ExitStack() as mixer:
            qkvo = sb("qkvo", [P, 25, N], stack=mixer)
            with ExitStack() as lam:
                lg = sb("lg", [GP, 20, P], stack=lam)
                dt2 = sb("dt2", [GP, 2, 2], stack=lam)
                vrow = sb("vrow", [56, P], stack=lam)
                nrow = sb("nrow", [32, P], stack=lam)
                craw = sb("craw", [P, 2, KT, 2, SP], stack=lam)
            OT = sb("OT", [P, 5, E1], stack=mixer)
            Htok = sb("Htok", [P, 5, DV], stack=mixer)
            Qblk = sb("Qblk", [P, 320], stack=mixer)
            Kws = sb("Kws", [P, 2, 5, DK], stack=mixer)
            Kblk = sb("Kblk", [TS, 2, B, DK], stack=mixer)
            CP = sb("CP", [DK, 2, DV], stack=mixer)
            TK = sb("TK", [P, 5, P], stack=mixer)
            EX = sb("EX", [P, 5, 96], stack=mixer)
            SEL = sb("SEL", [8, H, P], stack=mixer)
            Msk = sb("Msk", [TS, TS], stack=mixer)
            MB = sb("MB", [TS, B], stack=mixer)
            st5 = sb("st5", [P, 8, 5], stack=mixer)
            Is = sb("Is", [TS, E1], stack=mixer)
        with ExitStack() as s5_mem:
            EC = sb("EC", [P, GP, SP], stack=s5_mem)
            ES = sb("ES", [P, GP, SP], stack=s5_mem)
            bb = sb("bb", [P, 2, GP, GC], stack=s5_mem)
            PW = sb("PW", [P, 3, T + 1, GP], stack=s5_mem)
            CA = sb("CA", [P, 2, GP, T + 1, GC], stack=s5_mem)
            CT = CA[:].rearrange("p r g j c -> p (r g j c)")
            srow = sb("srow", [P, 4, P], stack=s5_mem)
            prow = sb("prow", [2 * GP, P], stack=s5_mem)
            h0 = sb("h0", [P, 2, B, GP], stack=s5_mem)
            with ExitStack() as ffn_mem:
                rbuf = sb("rbuf", [P, N], stack=ffn_mem)
                tbuf = sb("tbuf", [P, N], stack=ffn_mem)
                qbuf = sb("qbuf", [P, N], stack=ffn_mem)
                braw = sb("braw", [P, 2, GP, GC], stack=ffn_mem)
                braw_row = braw[:, 1].rearrange("p g c -> p (g c)")
                dsel = braw_row[:, 96:112]
                dterm = braw[:, 0, 0:KT, :]
                ptmp = sb("ptmp", [P, 2, N], stack=ffn_mem)
            rowsel = ptmp[:, 0, 0:11 * GC]
            with ExitStack() as s5_run:
                GS = sb("GS", [P, 2, 4, T * GC], stack=s5_run)
                gtmp = sb("gtmp", [P, 4, T * GC], stack=s5_run)
                rot = sb("rot", [P, 4, 4, SP], stack=s5_run)
                rho = sb("rho", [P, 4, SP], stack=s5_run)
                Hst = sb("Hst", [P, 2, 2, 4, COLS + 1], stack=s5_run)
                hP = sb("hP", [P, 2, GP], stack=s5_run)
                R2 = sb("R2", [P, COLS], stack=s5_run)
            with ExitStack() as glu_mem:
                gbuf = sb("gbuf", [P, N], stack=glu_mem)
                sbuf = sb("sbuf", [P, N], stack=glu_mem)
                tb2 = sb("tb2", [P, N], stack=glu_mem)
                ys = sb("ys", [TS, D], stack=glu_mem)
        E = qkvo[:, 16 - KT:16, :].rearrange("p a n -> p (a n)")[:, 0:2688].rearrange("p (s n) -> p s n", s=2)
        Es = qkvo[0:TS, 16 - KT:16, :].rearrange("p a n -> p (a n)")[:, 2688:2688 + H * TS]
        xg_stack.close()
        with ExitStack() as att:
            Vtok = sb("Vtok", [P, 5, H, E1], stack=att)
            Ktok = sb("Ktok", [P, 5, 4, P], stack=att)
            Cst = sb("Cst", [P, 2, 4, E1], stack=att)
        with ExitStack() as s5_a:
            U2 = sb("U2", [P, G, COLS], stack=s5_a)
            with ExitStack() as un_mem:
                unat = sb("unat", [P, KT, N], stack=un_mem)
            GT = sb("GT", [P, 2, 8, P], stack=s5_a)
            MT = sb("MT", [P, 2, 8, P], stack=s5_a)
            hN = sb("hN", [P, 2, B, GP], stack=s5_a)
        yn, yv = (sqb[:], R[:]), acc
        taps_of = [MT[:, k % 2] for k in range(KT - 2)] + [
            late[:, i, KT - 2:KT].rearrange("p a n -> p (a n)")[:, 0:8 * P].rearrange("p (g m) -> p g m", g=8) for i in range(2)]
        gains_by = (GS[:], cT[:].rearrange("p r (q j) c -> p r q (j c)", q=4))
        with ExitStack() as taps_mem:
            bblk = sb("bblk", [P, 2, GP, 2, GC], stack=taps_mem)
            ktap = sb("ktap", [P, KT, TAPS], stack=taps_mem)
        with ExitStack() as fin_mem:
            xf = sb("xf", [P, KT, N], stack=fin_mem)
            ybuf = sb("ybuf", [P, NB, D], stack=fin_mem)
        finished = [ys] + [ybuf[:, i] for i in range(NB)]
        ps = ctx.enter_context(nc.psum_tensor("ps", [P, 8, 512], F32))

        def halves(ap):
            return ap.rearrange("p (n c) -> p n c", n=2)

        def steps(ap):
            return ap.rearrange("p (t b) -> p b t", t=T)

        def blocks(ap):
            return ap.rearrange("p (b t) -> p b t", t=T)

        def slab_ps(s):
            return ps[:, 2 * s:2 * s + 2, 0:HN]

        def sems(names):
            return [ctx.enter_context(nc.semaphore(n)) for n in names.split()]

        (x_in, vec_in, lam_in, craw_in, nrow_in, gate_in, b_in, st5_in) = sems(
            "x_in vec_in lam_in craw_in nrow_in gate_in b_in st5_in")
        (dve_step, act_step, pool_step) = sems(
            "dve_step act_step pool_step")
        (const_done, xt_done, x_ready, vec_pe, vec_ready, lam_pe, lam_act, lam_dve, craw_pe, craw_ready) = sems(
            "const_done xt_done x_ready vec_pe vec_ready lam_pe lam_act lam_dve craw_pe craw_ready")
        (whi_done, w_ready, slab_done) = sems(
            "whi_done w_ready slab_done")
        (sq_done, sq0_done, sq7_done, acc_done, xhi_done, xg_ready, stat_done, rms_done, R_ready) = sems(
            "sq_done sq0_done sq7_done acc_done xhi_done xg_ready stat_done rms_done R_ready")
        (scaled, squared, hhi_done, hid_ready) = sems(
            "scaled squared hhi_done hid_ready")
        (gate_pe, gate_act, am_ready, q4_clear, q4_ready, m_ready, dec_rhs, tk_pe, ex_ready) = sems(
            "gate_pe gate_act am_ready q4_clear q4_ready m_ready dec_rhs tk_pe ex_ready")
        (att_const, kv_done, kv_act, kv_dve, osig_act, osig_ready, us_done, us_arg, us_exp, es_ready) = sems(
            "att_const kv_done kv_act kv_dve osig_act osig_ready us_done us_arg us_exp es_ready")
        (u_done, s_done, exp_done, p_done, p_masked) = sems(
            "u_done s_done exp_done p_done p_masked")
        (qblk_ready, ncol_ready, pv_done, ot_act, ot_ready, ssq_done, ms_ready, rstd_ready, htok_ready,
         ht_done, hf_ready) = sems(
            "qblk_ready ncol_ready pv_done ot_act ot_ready ssq_done ms_ready rstd_ready htok_ready ht_done "
            "hf_ready")
        (kws_ready, upa_done, upb_done, cb_done, c_new, n_pe, n_rows) = sems(
            "kws_ready upa_done upb_done cb_done c_new n_pe n_rows")
        (bb_done, pool_pre, taps_done, kt_act, taps_set, taps_out, h0_act) = sems(
            "bb_done pool_pre taps_done kt_act taps_set taps_out h0_act")
        (u_ready, u_out, row_sel, r2_pe, r2_act, r2_ready, un_ready) = sems(
            "u_ready u_out row_sel r2_pe r2_act r2_ready un_ready")
        (s5_set, gs_ready, gt_done, gt_ready, v_done, h_ready, hst_ready, sy_done, yev_ready, gel_done) = sems(
            "s5_set gs_ready gt_done gt_ready v_done h_ready hst_ready sy_done yev_ready gel_done")
        (ssend_pe, ssend_rows, sig_done, glu_done) = sems(
            "ssend_pe ssend_rows sig_done glu_done")
        (fin_pe, fin_act, fin_ready, xf_ready, yt_done, y_act, y_dve, y_out, out_done) = sems(
            "fin_pe fin_act fin_ready xf_ready yt_done y_act y_dve y_out out_done")
        raw_in, ps_free, c_in, c_out, u2_in, mt_in, late_in, yn_in, y2_out = (
            [ctx.enter_context(nc.semaphore(f"{n}{s}")) for s in range(2)]
            for n in ("raw_in", "ps_free", "c_in", "c_out", "u2_in", "mt_in", "late_in", "yn_in", "y2_out"))

        class Steps:

            def __init__(self, eng, own):
                self.eng, self.own, self.n = eng, own, 0

            def link(self, ins):
                self.n += 1
                ins.then_inc(self.own, 1)
                self.eng.wait_ge(self.own, self.n)

        def load_slab(sp, base, j, src):
            s = base % 2
            if base >= 2:
                sp.wait_ge(w_ready, base - 1 + 2 * j)
            sp.dma_start(raw[:, s], src).then_inc(raw_in[s], 16)

        def split_hi(act, base, j):
            s = base % 2
            if base >= 2:
                act.wait_ge(slab_done, base - 1 + 2 * j)
            act.wait_ge(raw_in[s], 16 * (base // 2 + 1) + 16 * j)
            nc.scalar.activation(whi[:, s], raw[:, s], ACT.Copy).then_inc(whi_done, 1)

        def split_lo(dve, base, j):
            s = base % 2
            dve.wait_ge(whi_done, base + 1 + 2 * j)
            nc.vector.tensor_tensor(wlo[:, s], raw[:, s], whi[:, s].bitcast(F32),
                                    ALU.subtract).then_inc(w_ready, 1)

        def product(pe, base, j, rhs, ready=None, ks=range(KT)):
            s = base % 2
            hi, lo = rhs
            if 0 in ks:
                pe.wait_ge(w_ready, base + 1 + 2 * j)
                if base >= 2:
                    pe.wait_ge(ps_free[s], base // 2 + j)
            for k in ks:
                if ready:
                    pe.wait_ge(ready[0], ready[1] + k + 1)
                for n, (w, a) in enumerate(((whi, hi), (whi, lo), (wlo, hi))):
                    for c in range(2):
                        last = nc.tensor.matmul(ps[:, 2 * s + c, 0:HN], w[:, s, k, :],
                                                a[:, k, c * HN:(c + 1) * HN],
                                                start=(k == 0 and n == 0), stop=(k == KT - 1 and n == 2))
            if KT - 1 in ks:
                last.then_inc(slab_done, 1)

        def stats(pe, stage):
            pe.wait_ge(acc_done, ACC0[stage + 1])
            for c in range(2):
                last = nc.tensor.matmul(ps[:, 4 + c, 0:HN], ones[:], acc[:, c * HN:(c + 1) * HN],
                                        start=True, stop=True)
            last.then_inc(stat_done, 1)

        def rms(act, n):
            act.wait_ge(stat_done, n + 1)
            nc.scalar.activation(halves(R[:]), ps[:, 4:6, 0:HN], ACT.Sqrt, bias=eps[:, 0:1],
                                 scale=1.0 / D).then_inc(rms_done, 1)

        def inv_rms(dve, n):
            dve.wait_ge(rms_done, n + 1)
            nc.vector.reciprocal(R[:], R[:]).then_inc(R_ready, 1)
            dve.wait_ge(R_ready, n + 1)

        def gain(v, k):
            return vec[:, v, k:k + 1] if isinstance(k, int) else vec[:, v, bass.ds(k, 1)]

        def tile(a, k):
            return a[:, k] if isinstance(k, int) else a[:, bass.ds(k, 1), :].rearrange("p a n -> p (a n)")

        X_SLABS = {1: (I_OUT, 1), 2: (I_FFN[0] + 56, 1), 3: (I_GLU + 1, 2), 4: (I_FFN[1] + 56, 1)}

        def wait_x(eng, stage, q, j=0):
            if stage == 0:
                eng.wait_ge(x_ready, q + 1)
            else:
                base, step = X_SLABS[stage]
                base += step * q
                eng.wait_ge(ps_free[base % 2], base // 2 + 1 + step * j)

        def prep_hi(act, q, j, stage, n, v):
            wait_x(act, stage, q, j)
            k = q + 2 * j
            nc.scalar.activation(tile(xg_hi, k), tile(x, k), ACT.Identity,
                                 scale=gain(v, k)).then_inc(xhi_done, 1)

        def prep_lo(dve, k, n, v):
            dve.wait_ge(xhi_done, KT * n + 1 + k)
            nc.vector.scalar_tensor_tensor(tile(xg_lo, k), tile(x, k), gain(v, k), tile(xg_hi, k).bitcast(F32),
                                           ALU.mult, ALU.subtract).then_inc(xg_ready, 1)

        sq0 = (sqb[:], qkvo[:, 23])
        ACC0 = (0, 8, 16, 23, 31, 38)

        def square_sums(pool, stage):
            n0 = ACC0[stage]
            if stage:
                wait_x(pool, stage, 0)
                nc.gpsimd.tensor_tensor(acc[:], x[:, 0], x[:, 0], ALU.mult).then_inc(acc_done, 1)
            for k in range(1, ACC0[stage + 1] - n0):
                pool.wait_ge(acc_done, n0 + k)
                if stage:
                    wait_x(pool, stage, k)
                    nc.gpsimd.tensor_tensor(sqb[:], x[:, k], x[:, k], ALU.mult).then_inc(sq_done, 1)
                    pool.wait_ge(sq_done, n0 - KT - (stage - 1) + k)
                    sq = sqb[:]
                else:
                    pool.wait_ge(sq0_done, k)
                    sq = sq0[k % 2]
                nc.gpsimd.tensor_tensor(acc[:], acc[:], sq, ALU.add).then_inc(acc_done, 1)

        def last_squares(dve, stage):
            wait_x(dve, stage, KT - 1)
            nc.vector.tensor_tensor(R[:], x[:, KT - 1], x[:, KT - 1], ALU.mult).then_inc(sq7_done, 1)

        GB = (6, 2, 0, 2, 0, 2, 0, 2)
        GELUS = {4: (0,), 5: (1,), 6: (2,), 7: (3, 4), 8: (5,), 9: (6,), 10: (7,)}
        GELU_LOS = {4: (0,), 5: (1,), 7: (2, 3, 4), 8: (5,), 9: (6,), 10: (7,)}
        YB = (0, 2, 6, 0, 2)
        OFF = [0, 512, 1024, 896]
        block = ctx.enter_context(nc.Block())

        @block.sync
        def _(sp):
            sp.dma_start(xtok[0:TS, 0, :], x_sample.rearrange("b t d -> (b t) d")).then_inc(x_in, 16)
            for i in range(NB):
                sp.dma_start(xtok[:, 1 + i, :], x_prompt[0, i * P:(i + 1) * P, :]).then_inc(x_in, 16)
            load_slab(sp, 0, 0, slab_in[:, :, 24 * P + 16 - P:24 * P + 16])
            load_slab(sp, 1, 0, slab_in[:, :, 0:P])
            for b4 in range(4):
                for b2 in range(2):
                    sp.dma_start(nrow[b4 * 8:b4 * 8 + 8, b2 * DK:(b2 + 1) * DK],
                                 st_n[0, 2 * b4 + b2]).then_inc(nrow_in, 16)
            with nc.allow_non_contiguous_dma(reason="80 numbers"):
                sp.dma_start(gs[:, M0:M0 + B], st_m[0].rearrange("b h -> h b")).then_inc(gate_in, 16)
                sp.dma_start(gs[:, BI:BI + 1], b_i.rearrange("a h -> h a")).then_inc(gate_in, 16)
                sp.dma_start(gs[:, BF:BF + 1], b_f.rearrange("a h -> h a")).then_inc(gate_in, 16)
            for ri, a in enumerate((c_re, c_im)):
                for dup in range(2):
                    sp.dma_start(craw[:, ri, :, dup, :],
                                 a[0].rearrange("(k g) c p -> (g c) k p", g=8)).then_inc(craw_in, 16)
            load_slab(sp, 2, 0, slab_in[:, :, P:2 * P])
            load_slab(sp, 3, 0, slab_in[:, :, 2 * P:3 * P])
            with sp.Fori(0, 10) as j:
                for q in range(2):
                    load_slab(sp, 4 + q, j, slab_in[:, :, bass.ds((3 + q) * P + j * (2 * P), P)])
            load_slab(sp, 24, 0, slab_in[:, :, 23 * P:24 * P])
            load_slab(sp, 25, 0, slab_out[:, :, 0:P])
            for c in range(1, 4):
                load_slab(sp, 25 + c, 0, slab_out[:, :, c * P:(c + 1) * P])

            def load_state(h):
                s = h % 2
                if h < 2:
                    sp.wait_ge(slab_done, 25)
                else:
                    sp.wait_ge(c_out[s], 16 * 3 * (h // 2))
                for b2 in range(2):
                    sp.dma_start(Cst[b2 * DK:(b2 + 1) * DK, s, :, 0:DV],
                                 st_C[0, b2::2, h].rearrange("b d e -> d b e")).then_inc(c_in[s], 16)

            load_state(0)
            load_state(1)
            sp.wait_ge(m_ready, 1)
            with nc.allow_non_contiguous_dma(reason="72 numbers"):
                sp.dma_start(s_m[0].rearrange("b h -> h b"), gs[:, MPT:MPT + B]).then_inc(out_done, 16)
                sp.dma_start(p_m[0].rearrange("b h -> h b"), gs[:, MPT + B:MPT + B + 1]).then_inc(out_done, 16)
            for h in range(H):
                s = h % 2
                sp.wait_ge(c_new, h + 1)
                for b2 in range(2):
                    sp.dma_start(s_C[0, b2::2, h].rearrange("b d e -> d b e"),
                                 Cst[b2 * DK:(b2 + 1) * DK, s, :, 0:DV]).then_inc(c_out[s], 16)
                sp.dma_start(p_C[0, 0, h], CP[:, s, :]).then_inc(c_out[s], 16)
                if h + 2 < H:
                    load_state(h + 2)
            sp.wait_ge(n_rows, 1)
            for b4 in range(4):
                for b2 in range(2):
                    sp.dma_start(s_n[0, 2 * b4 + b2], TK[b4 * 8:b4 * 8 + 8, 0, b2 * DK:(b2 + 1) * DK]).then_inc(out_done, 16)
            sp.dma_start(p_n[0, 0], TK[0:H, 1, 0:DK]).then_inc(out_done, 16)
            for c in range(4, KT):
                load_slab(sp, 25 + c, 0, slab_out[:, :, c * P:(c + 1) * P])

            def ffn_loads(l):
                up, down = I_FFN[l], I_FFN[l] + 8
                with sp.Fori(0, 4) as j:
                    for q in range(2):
                        load_slab(sp, up + q, j, slab_up[l][:, :, bass.ds(q * P + j * (2 * P), P)])
                with sp.Fori(0, FF - 1) as f:
                    with sp.Fori(0, 4) as j:
                        for q in range(2):
                            load_slab(sp, down + q, 8 * f + j, slab_down[l][:, bass.ds(f, 1), :, bass.ds(q * P + j * (2 * P), P)]
                                      .rearrange("p f k c -> p (f k) c"))
                    with sp.Fori(0, 4) as j:
                        for q in range(2):
                            load_slab(sp, up + 16 + q, 8 * f + j, slab_up[l][:, :, bass.ds((D + q * P) + f * D + j * (2 * P), P)])
                if l == 0:
                    for q in range(2):
                        load_slab(sp, down + 48 + q, 0, slab_down[l][:, FF - 1, :, q * P:(q + 1) * P])
                    return
                with sp.Fori(0, 4) as j:
                    for q in range(2):
                        load_slab(sp, down + 48 + q, j, slab_down[l][:, FF - 1, :, bass.ds(q * P + j * (2 * P), P)])

            sp.wait_ge(out_done, 16 * 11)
            for s in range(2):
                sp.wait_ge(c_out[s], 16 * 3 * 4)
            for ri, a in enumerate((b_re, b_im)):
                for g2 in range(2):
                    sp.dma_start(braw[g2 * SP:(g2 + 1) * SP, ri],
                                 a[0].rearrange("(a b) p c -> b p a c", b=2)[g2]).then_inc(b_in, 16)
            for hf in range(2):
                for ri, a in enumerate((st_re, st_im)):
                    sp.dma_start(srow[:, 2 * ri + hf, :],
                                 a[0].rearrange("b (a g) p -> (b a) (g p)", g=2)[hf * P:(hf + 1) * P]).then_inc(st5_in, 16)
            ffn_loads(0)

            def load_u(half):
                sp.wait_ge(u_out, 16 * 4 * (half + 1))
                g = slice(half * G // 2, (half + 1) * G // 2)
                for i in range(T):
                    sp.dma_start(U2[i * GC:(i + 1) * GC, g, :],
                                 d_u.rearrange("(g c) t b -> t c g b", c=GC)[T - 1 - i, :, g]).then_inc(u2_in[half], 16)

            for k in range(KT):
                if k < 6:
                    load_slab(sp, I_FFN[0] + 58 + k, 0, slab_down[0][:, FF - 1, :, (k + 2) * P:(k + 3) * P])
                else:
                    load_slab(sp, I_GLU + k - 6, 0, slab_glu[:, :, D * (7 - k):D * (7 - k) + P])
                if k == 4:
                    sp.wait_ge(taps_out, 16)
                    load_u(0)
                sp.wait_ge(u_ready, k + 1)
                sp.dma_start(d_u[k * P:(k + 1) * P].rearrange("p t b -> p (t b)"), unat[:, k]).then_inc(u_out, 16)
                if k == 3:
                    sp.wait_ge(taps_set, 1)
                    sp.dma_start(d_taps.rearrange("(k p) c -> p k c", p=P), ktap[:]).then_inc(taps_out, 16)
            load_u(1)

            def load_taps(k):
                s = k % 2
                if 2 <= k < KT - 2:
                    sp.wait_ge(sy_done, k - 1)
                for i in range(T):
                    sp.dma_start(taps_of[k][i * GC:(i + 1) * GC],
                                 d_taps[k * P:(k + 1) * P, i * GC:i * GC + P].rearrange("(g c) m -> c g m", c=GC)).then_inc(mt_in[s] if k < KT - 2 else late_in[s], 16)

            load_taps(0)
            load_taps(1)
            sp.wait_ge(slab_done, I_GLU)
            load_taps(KT - 2)
            load_taps(KT - 1)
            groups = ((0, 1), (2, 3), (4,), (5,), (6,), (7,))

            def fetch_y(n):
                sp.wait_ge(y2_out[n % 2], 16 * T * (n // 2 + 1))
                for k in groups[n]:
                    if k >= 2:
                        sp.wait_ge(gel_done, k - 1)
                    if k == 1:
                        sp.wait_ge(r2_pe, 1)
                    sp.dma_start(yn[k % 2], d_y[k * P:(k + 1) * P].rearrange("p t b -> p (t b)")).then_inc(yn_in[k % 2], 16)

            for n, group in enumerate(groups):
                for k in group:
                    if k + 2 < KT - 2:
                        load_taps(k + 2)
                first, last = group[0], group[-1]
                sp.wait_ge(yev_ready, last + 1)
                for i in range(T):
                    sp.dma_start(d_y[first * P:(last + 1) * P].rearrange("(g c) t b -> t c g b", c=GC)[i],
                                 U2[i * GC:(i + 1) * GC, 8 * first:8 * last + 8, :]).then_inc(y2_out[n % 2], 16)
                fetch_y(n)
            for i in range(2):
                load_slab(sp, I_GLU + 2 + i, 0, slab_glu[:, :, P + D * (1 - i):2 * P + D * (1 - i)])
            sp.wait_ge(ssend_rows, 1)
            for hf in range(2):
                for ri, a in enumerate((s_re, s_im)):
                    sp.dma_start(a[0].rearrange("b (a g) p -> (b a) (g p)", g=2)[hf * P:(hf + 1) * P],
                                 srow[:, 2 * ri + hf, :]).then_inc(out_done, 16)
            for ri, a in enumerate((p_re, p_im)):
                sp.dma_start(a[0, 0].rearrange("(a g) p -> a (g p)", g=2), prow[ri * GP:(ri + 1) * GP, :]).then_inc(out_done, 16)
            with sp.Fori(0, 6) as j:
                for i in range(2):
                    load_slab(sp, I_GLU + 4 + i, j, slab_glu[:, :, bass.ds(2 * P + D * (1 - i) + j * P, P)])
            ffn_loads(1)
            for i in range(5):
                sp.wait_ge(y_act, i + 1)
                sp.wait_ge(y_dve, i + 1)
                out = y_sample.rearrange("b t d -> (b t) d") if i == 0 else y_prompt[0, (i - 1) * P:i * P, :]
                sp.dma_start(out, finished[i][:, :]).then_inc(y_out, 16)
            sp.wait_ge(y_out, 16 * 5)
            sp.wait_ge(out_done, 16 * 17)
            sp.wait_ge(c_out[0], 16 * 3 * 4)
            sp.wait_ge(c_out[1], 16 * 3 * 4)

        @block.gpsimd
        def _(pool):
            own = Steps(pool, pool_step)
            own.link(nc.gpsimd.memset(ident[:], 0.0))
            nc.gpsimd.affine_select(out=ident[:], in_=ident[:], compare_op=ALU.not_equal, fill=1.0, base=0,
                                    pattern=[[-1, P]], channel_multiplier=1).then_inc(const_done, 1)
            nc.gpsimd.memset(ones[:], 1.0)
            nc.gpsimd.memset(gs[:, 8:9], 0.0)
            nc.gpsimd.memset(eps[:], EPS).then_inc(const_done, 1)
            own.link(nc.gpsimd.memset(gw[:, AM, :], 1.0))
            nc.gpsimd.memset(gw[:, AM, 0:TS + 1:T], 0.0).then_inc(am_ready, 1)
            square_sums(pool, 0)
            pool.wait_ge(xt_done, KT)
            nc.gpsimd.memset(Q4, 0.0).then_inc(q4_clear, 1)
            pool.wait_ge(q4_clear, 1)
            pool.wait_ge(craw_ready, 3)
            own.link(nc.gpsimd.memset(SEL[:], 1.0))
            nc.gpsimd.affine_select(out=SEL[:], in_=SEL[:], compare_op=ALU.is_equal, fill=0.0, base=0,
                                    pattern=[[-1, H], [0, P]], channel_multiplier=1)
            nc.gpsimd.memset(Qblk[:], 0.0)
            nc.gpsimd.memset(OT[:], 0.0)
            nc.gpsimd.memset(TK[:], 0.0)
            own.link(nc.gpsimd.memset(MB[:], 1.0))
            own.link(nc.gpsimd.affine_select(out=MB[:], in_=MB[:], compare_op=ALU.is_ge, fill=0.0, base=0,
                                             pattern=[[-T, B]], channel_multiplier=1))
            own.link(nc.gpsimd.affine_select(out=MB[:], in_=MB[:], compare_op=ALU.is_ge, fill=0.0, base=T - 1,
                                             pattern=[[T, B]], channel_multiplier=-1))
            own.link(nc.gpsimd.tensor_copy(Msk[:].rearrange("s (b t) -> s b t", b=B),
                                           MB[:].unsqueeze(2).to_broadcast([TS, B, T])))
            nc.gpsimd.affine_select(out=Msk[:], in_=Msk[:], compare_op=ALU.is_ge, fill=0.0, base=0,
                                    pattern=[[1, TS]], channel_multiplier=-1).then_inc(att_const, 1)
            pool.wait_ge(slab_done, 25)
            nc.gpsimd.memset(Vtok[:, :, :, DV:E1], 1.0).then_inc(att_const, 1)
            pool.wait_ge(osig_act, 1)
            for h in range(H):
                nc.gpsimd.tensor_scalar(qkvo[:, 16 + h], qkvo[:, 16 + h], 1.0, 0.5, ALU.add, ALU.mult).then_inc(osig_ready, 1)

            def mask(h):
                e = E[:, h % 2]
                pool.wait_ge(p_done, h + 1)
                for j in range(NB):
                    blk = e[:, OFF[j]:OFF[j] + P]
                    last = nc.gpsimd.affine_select(out=blk, in_=blk, compare_op=ALU.is_ge, fill=0.0, base=0,
                                                   pattern=[[1, P]], channel_multiplier=-1)
                last.then_inc(p_masked, 1)

            def n_column(h):
                pool.wait_ge(c_in[h % 2], 32 * (h // 2 + 1))
                nc.gpsimd.tensor_copy(Cst[:, h % 2, :, DV], nT[:].rearrange("p (b h) -> p b h", b=4)[:, :, h]).then_inc(ncol_ready, 1)

            pool.wait_ge(us_exp, 1)
            es = Es.rearrange("s (h t) -> s h t", h=H)
            nc.gpsimd.tensor_tensor(es, es, Msk[:].unsqueeze(1).to_broadcast([TS, H, TS]), ALU.mult).then_inc(es_ready, 1)
            def sample_queries(h):
                if h:
                    pool.wait_ge(pv_done, h)
                hp = h % 2 * DK
                for b2 in range(2):
                    last = nc.gpsimd.tensor_copy(
                        Qblk[b2 * DK:(b2 + 1) * DK, :].rearrange("p (b c) -> p b c", b=4)[:, :, b2 * T:(b2 + 1) * T],
                        qkvo[hp:hp + DK, h // 2, 0:TS].rearrange("p (b a t) -> p b a t", a=2, t=T)[:, :, b2, :])
                    if not b2:
                        own.link(last)
                last.then_inc(qblk_ready, 1)
                pool.wait_ge(qblk_ready, h + 1)

            def keys(h):
                s = h % 2
                if h >= 2:
                    pool.wait_ge(upb_done, h - 1)
                kc = slice(h % 2 * DK, (h % 2 + 1) * DK)
                own.link(nc.gpsimd.tensor_tensor(Kws[0:TS, s, 0, :], Ktok[0:TS, 0, h // 2, kc],
                                                 EX[0:TS, 0, h:h + 1].to_broadcast([TS, DK]), ALU.mult))
                own.link(nc.gpsimd.tensor_tensor(Kws[:, s, 1:5, :], Ktok[:, 1:5, h // 2, kc],
                                                 EX[:, 1:5, h:h + 1].to_broadcast([P, NB, DK]), ALU.mult))
                nc.gpsimd.tensor_tensor(Kblk[:, s], Kws[0:TS, s, 0, :].unsqueeze(1).to_broadcast([TS, B, DK]),
                                        MB[:].unsqueeze(2).to_broadcast([TS, B, DK]), ALU.mult).then_inc(kws_ready, 1)

            pool.wait_ge(ex_ready, 2)
            own.link(nc.gpsimd.tensor_scalar(EX[:, :, 0:H], EX[:, :, 0:H], DK ** -0.5, None, ALU.mult))
            pool.wait_ge(kv_act, 6)
            pool.wait_ge(kv_dve, 6)
            keys(0)
            sample_queries(0)
            n_column(0)
            mask(0)
            for h in range(H + 1):
                if h:
                    pool.wait_ge(ms_ready, h)
                    nc.gpsimd.tensor_tensor(st5[:, 5, :], st5[:, 4, :], st5[:, 6, :], ALU.pow).then_inc(rstd_ready, 1)
                if h + 1 < H:
                    mask(h + 1)
                    keys(h + 1)
                    sample_queries(h + 1)
                    n_column(h + 1)
            square_sums(pool, 1)

            def cmul(out_re, out_im, a, b, tmp):
                t = nc.gpsimd.tensor_tensor
                t(tmp[0], a[0], b[0], ALU.mult)
                own.link(t(tmp[1], a[1], b[1], ALU.mult))
                own.link(t(out_re, tmp[0], tmp[1], ALU.subtract))
                t(tmp[0], a[0], b[1], ALU.mult)
                own.link(t(tmp[1], a[1], b[0], ALU.mult))
                own.link(t(out_im, tmp[0], tmp[1], ALU.add))

            pool.wait_ge(out_done, 16 * 11)
            for s in range(2):
                pool.wait_ge(c_out[s], 16 * 3 * 4)
            pool.wait_ge(hid_ready, 8)
            coef = [s5s[:, n, :].unsqueeze(2).to_broadcast([P, GP, GC]) for n in (CF_RE, CF_IM)]
            nc.gpsimd.tensor_copy(EC[:, :, 0], s5s[:, COS8, :])
            own.link(nc.gpsimd.tensor_copy(ES[:, :, 0], s5s[:, SIN8, :]))
            n = 1
            while n < SP:
                step = [t[:, :, n - 1:n].to_broadcast([P, GP, n]) for t in (EC, ES)]
                tmp = [CT[:, i * GP * 32:i * GP * 32 + GP * n].rearrange("p (g c) -> p g c", c=n) for i in range(2)]
                cmul(EC[:, :, n:2 * n], ES[:, :, n:2 * n], (EC[:, :, 0:n], ES[:, :, 0:n]), step, tmp)
                n *= 2
            nc.gpsimd.memset(PW[:, 0, 0, :], 1.0)
            nc.gpsimd.memset(PW[:, 1, 0, :], 0.0)
            nc.gpsimd.tensor_copy(PW[:, 0, 1, :], s5s[:, A_RE, :])
            own.link(nc.gpsimd.tensor_copy(PW[:, 1, 1, :], s5s[:, A_IM, :]))
            for m in (1, 2, 4):
                step = [PW[:, i, m:m + 1, :].to_broadcast([P, m, GP]) for i in range(2)]
                tmp = [ptmp[:, i, 0:m * GP].rearrange("p (m g) -> p m g", m=m) for i in range(2)]
                cmul(PW[:, 0, m + 1:2 * m + 1, :], PW[:, 1, m + 1:2 * m + 1, :],
                     (PW[:, 0, 1:m + 1, :], PW[:, 1, 1:m + 1, :]), step, tmp)
            own.link(nc.gpsimd.tensor_scalar(PW[:, 2], PW[:, 1], -1.0, None, ALU.mult))
            pool.wait_ge(b_in, 64)
            tmp = [ptmp[:, i, 0:GP * GC].rearrange("p (g c) -> p g c", g=GP) for i in range(2)]
            cmul(bb[:, 0], bb[:, 1], coef, (braw[:, 0], braw[:, 1]), tmp)
            own.link(nc.gpsimd.tensor_tensor(braw_row[:, 0:64], ident[:, 0:64], ident[:, 64:128], ALU.add))
            own.link(nc.gpsimd.tensor_tensor(braw_row[:, 64:96], braw_row[:, 0:32], braw_row[:, 32:64], ALU.add))
            own.link(nc.gpsimd.tensor_tensor(dsel, braw_row[:, 64:80], braw_row[:, 80:96], ALU.add))
            own.link(nc.gpsimd.tensor_tensor(dterm, dsel.unsqueeze(1).to_broadcast([P, KT, GC]),
                                             vec[:, V_SKIP, :].unsqueeze(2).to_broadcast([P, KT, GC]), ALU.mult))
            for k in range(KT):
                g = slice(4 * k, 4 * k + 4)
                c = [cT[:, ri, g, :].unsqueeze(2).to_broadcast([P, 4, T + 1, GC]) for ri in range(2)]
                a = [PW[:, v, :, g].rearrange("p j g -> p g j").unsqueeze(3).to_broadcast([P, 4, T + 1, GC]) for v in range(3)]
                tmp = [ptmp[:, i].rearrange("p (g j c) -> p g j c", g=4, c=GC) for i in range(2)]
                t = nc.gpsimd.tensor_tensor
                t(tmp[0], c[0], a[0], ALU.mult)
                own.link(t(tmp[1], c[1], a[1], ALU.mult))
                own.link(t(CA[:, 0, g], tmp[0], tmp[1], ALU.subtract))
                t(tmp[0], c[0], a[2], ALU.mult)
                own.link(t(tmp[1], c[1], a[0], ALU.mult))
                own.link(t(CA[:, 1, g], tmp[0], tmp[1], ALU.subtract))
            pool.wait_ge(slab_done, I_FFN[0] + 56)
            own.link(nc.gpsimd.memset(bblk[:], 0.0))
            own.link(nc.gpsimd.memset(ktap[:, :, 0:PAD], 0.0))
            for g2 in range(2):
                hf = slice(g2 * SP, (g2 + 1) * SP)
                last = nc.gpsimd.tensor_copy(bblk[hf, :, :, g2, :], bb[hf])
            last.then_inc(bb_done, 1)
            pool.wait_ge(bb_done, 1)

            def gains(k):
                g = slice(4 * k, 4 * k + 4)
                v = [bb[:, ri, g, :].unsqueeze(2).to_broadcast([P, 4, T, GC]) for ri in range(2)]
                a = [PW[:, ri, 0:T, g].rearrange("p j g -> p g j").unsqueeze(3).to_broadcast([P, 4, T, GC]) for ri in range(2)]
                gs = gains_by[k % 2]
                re, im, tmp = (t.rearrange("p g (j c) -> p g j c", c=GC) for t in (gs[:, 0], gs[:, 1], gtmp[:]))
                t = nc.gpsimd.tensor_tensor
                if k:
                    pool.wait_ge(gs_ready, k)
                if k >= 2:
                    pool.wait_ge(gt_done, k - 1)
                t(re, v[0], a[0], ALU.mult)
                own.link(t(tmp, v[1], a[1], ALU.mult))
                own.link(t(re, re, tmp, ALU.subtract))
                t(im, v[0], a[1], ALU.mult)
                own.link(t(tmp, v[1], a[0], ALU.mult))
                t(im, im, tmp, ALU.add).then_inc(gs_ready, 1)

            pool.wait_ge(hid_ready, HID0[0] + 32)
            gains(0)
            pool.wait_ge(kt_act, 2)
            own_tap = ktap[:, :, PAD:PAD + GC]
            nc.gpsimd.tensor_tensor(own_tap, own_tap, dterm, ALU.add).then_inc(taps_set, 1)
            gains(1)
            own.link(nc.gpsimd.memset(rowsel, 0.0))
            nc.gpsimd.memset(rowsel[:, 7 * GC:8 * GC], 1.0).then_inc(row_sel, 1)
            square_sums(pool, 2)
            pool.wait_ge(r2_pe, 1)
            own.link(nc.gpsimd.memset(Hst[:, :, :, :, B:B + 1], 0.0))
            nc.gpsimd.memset(rho[:], 0.0).then_inc(s5_set, 1)

            for k in range(2, KT):
                gains(k)
            pool.wait_ge(h_ready, KT)
            pool.wait_ge(gt_done, KT)
            pool.wait_ge(gs_ready, KT)
            a8 = [PW[:, ri, T:T + 1, :].to_broadcast([P, B, GP]) for ri in range(2)]
            tmp = [GS[:, i // 2, 2 * (i % 2):2 * (i % 2) + 2, :].rearrange("p a b -> p (a b)").rearrange("p (b g) -> p b g", b=B)
                   for i in range(4)]
            cmul(tmp[2], tmp[3], a8, (h0[:, 0], h0[:, 1]), tmp)
            for ri in range(2):
                last = nc.gpsimd.tensor_tensor(hN[:, ri], hN[:, ri], tmp[2 + ri], ALU.add)
                if not ri:
                    own.link(last)
            last.then_inc(pool_pre, 1)
            pool.wait_ge(pool_pre, 1)
            square_sums(pool, 3)
            square_sums(pool, 4)

        @block.scalar
        def _(act):
            own = Steps(act, act_step)
            act.dma_start(lg[:, 0, :], lam_re[0].rearrange("(a b) p -> a (b p)", b=2)).then_inc(lam_in, 16)
            act.dma_start(lg[:, 1, :], lam_im[0].rearrange("(a b) p -> a (b p)", b=2)).then_inc(lam_in, 16)
            act.dma_start(dt2[:, 0, :], log_dt[0].rearrange("(a b) -> a b", b=2)).then_inc(lam_in, 16)
            for v, a in ((V_MIX0, g_mix), (V_FFN0, g_ffn), (V_HEAD, g_head), (V_SKIP, s5_d)):
                n = a.shape[0] * KT
                act.dma_start(vrow[v * KT:v * KT + n, :], a.rearrange("v (k p) -> (v k) p", p=P)).then_inc(vec_in, 16)
            act.dma_start(vrow[V_FIN * KT:(V_FIN + 1) * KT, :], g_fin.rearrange("(k p) -> k p", p=P)).then_inc(vec_in, 16)
            act.wait_ge(lam_in, 48)
            nc.scalar.activation(dt2[:, 1, :], dt2[:, 0, :], ACT.Exp).then_inc(lam_act, 1)
            act.wait_ge(lam_dve, 1)
            nc.scalar.activation(lg[:, 4, :], lg[:, 2, :], ACT.Exp)
            nc.scalar.activation(lg[:, 16, :], lg[:, 2, :], ACT.Exp, scale=float(T)).then_inc(lam_act, 1)
            act.wait_ge(lam_dve, 2)
            nc.scalar.activation(lg[:, 10:12, :], lg[:, 7:9, :], ACT.Sin).then_inc(lam_act, 1)
            split_hi(act, 0, 0)
            split_hi(act, 1, 0)
            act.wait_ge(vec_ready, 1)
            for k in range(KT):
                prep_hi(act, k, 0, 0, 0, V_MIX0)
                if k == 0:
                    nc.scalar.activation(acc[:], x[:, 0], ACT.Square).then_inc(acc_done, 1)
                else:
                    if k >= 3:
                        act.wait_ge(acc_done, k - 1)
                    nc.scalar.activation(sq0[k % 2], x[:, k], ACT.Square).then_inc(sq0_done, 1)
            rms(act, 0)
            split_hi(act, 2, 0)
            split_hi(act, 3, 0)
            split_hi(act, 4, 0)
            act.wait_ge(gate_pe, 1)
            gz = halves(gw[:, GT1, :])
            act.wait_ge(gate_in, 48)
            own.link(nc.scalar.activation(gz, ps[0:8, 6:8, 0:HN], ACT.Abs, bias=gs[:, BF:BF + 1]))
            own.link(nc.scalar.activation(gw[:, GT1, :], gw[:, GT1, :], ACT.Exp, scale=-1.0))
            nc.scalar.activation(gw[:, GT1, :], gw[:, GT1, :], ACT.Ln, bias=ones[0:8, 0:1]).then_inc(gate_act, 1)
            split_hi(act, 5, 0)
            split_hi(act, 6, 0)
            act.wait_ge(m_ready, 1)
            nc.scalar.activation(gs[:, DEC:DEC + B], gs[:, DEC:DEC + B], ACT.Exp).then_inc(gate_act, 1)
            with act.Fori(1, 9) as j:
                for q in range(2):
                    split_hi(act, 5 + q, j)
            split_hi(act, 23, 0)
            split_hi(act, 24, 0)
            act.wait_ge(tk_pe, 1)
            act.wait_ge(att_const, 1)
            nc.scalar.activation(TK[0:TS, 0, :], ps[0:TS, 4, 0:P], ACT.Copy)
            own.link(nc.scalar.activation(TK[:, 1:5, :], ps[:, 5, :].rearrange("p (i c) -> p i c", i=NB), ACT.Copy))
            nc.scalar.activation(EX[:], TK[:, :, 32:P], ACT.Exp).then_inc(ex_ready, 1)
            own.link(nc.scalar.activation(dcy[0:DK], ps[0:DK, 6, 0:64].rearrange("p (h b c) -> p h b c", h=H, c=2)[:, :, :, 0], ACT.Copy))
            nc.scalar.activation(dcy[DK:P], ps[DK:P, 6, 0:64].rearrange("p (h b c) -> p h b c", h=H, c=2)[:, :, :, 1],
                                 ACT.Copy).then_inc(ex_ready, 1)
            act.wait_ge(ps_free[0], 12)
            act.wait_ge(ps_free[1], 11)
            nc.scalar.activation(qkvo[:, 16:22, :], qkvo[:, 16:22, :], ACT.Tanh, scale=0.5)
            split_hi(act, 25, 0)
            split_hi(act, 26, 0)
            act.wait_ge(ps_free[1], 12)
            act.wait_ge(ps_free[0], 13)
            nc.scalar.activation(qkvo[:, 22:24, :], qkvo[:, 22:24, :], ACT.Tanh, scale=0.5).then_inc(osig_act, 1)
            for i in range(0, 12, 2):
                act.wait_ge(kv_done, i + 1)
                r = 2 * (i % 4)
                if i < 4:
                    nc.scalar.activation(Ktok[:, 1:5, i, :], ps[:, r, :].rearrange("p (i c) -> p i c", i=NB), ACT.Copy)
                    nc.scalar.activation(Ktok[0:TS, 0, i, :], ps[0:TS, r + 1, 0:P], ACT.Copy).then_inc(kv_act, 1)
                else:
                    nc.scalar.activation(Vtok[:, 1:5, i - 4, 0:DV], ps[:, r, :].rearrange("p (i c) -> p i c", i=NB), ACT.Copy)
                    nc.scalar.activation(Vtok[0:TS, 0, i - 4, 0:DV], ps[0:TS, r + 1, 0:P], ACT.Copy).then_inc(kv_act, 1)

            def exps(h):
                e = E[:, h % 2]
                act.wait_ge(u_done, h + 1)
                if h >= 2:
                    act.wait_ge(pv_done, h - 1)
                for j in range(NB):
                    w = L - j * P
                    last = nc.scalar.activation(e[:, OFF[j]:OFF[j] + w], ps[:, 0, j * P:L], ACT.Exp, bias=TK[:, 1 + j, h:h + 1])
                last.then_inc(exp_done, 1)

            def head_hi(h):
                act.wait_ge(hf_ready, h + 1)
                nc.scalar.activation(hid_hi[:, h], qkvo[:, 16 + h], ACT.Copy).then_inc(hhi_done, 1)

            act.wait_ge(us_arg, 2)
            nc.scalar.activation(Es, Es, ACT.Exp).then_inc(us_exp, 1)
            exps(0)
            for h in range(H + 1):
                if h:
                    act.wait_ge(ot_ready, h)
                    if h > 1:
                        act.wait_ge(ht_done, h - 1)
                    for i in range(5):
                        last = nc.scalar.activation(Htok[:, i, :], OT[:, i, 0:DV], ACT.Square, accum_out=st5[:, 2, i:i + 1])
                    last.then_inc(ssq_done, 1)
                if h + 1 < H:
                    exps(h + 1)
                if h < H:
                    act.wait_ge(pv_done, h + 1)
                    if h:
                        act.wait_ge(htok_ready, h)
                    nc.scalar.activation(OT[:, 1:4, :], ps[:, 4, 0:3 * E1].rearrange("p (i c) -> p i c", i=3), ACT.Copy)
                    nc.scalar.activation(OT[:, 4, :], ps[:, 5, 0:E1], ACT.Copy)
                    nc.scalar.activation(Is[:], ps[0:TS, 5, 2 * E1:3 * E1], ACT.Copy, scale=EX[0:TS, 0, 64 + h:65 + h]).then_inc(ot_act, 1)
                if h:
                    head_hi(h - 1)
            act.wait_ge(n_pe, 1)
            nc.scalar.activation(TK[0:32, 0, :], ps[0:32, 6, 256:384], ACT.Copy)
            nc.scalar.activation(TK[0:H, 1, 0:DK], ps[0:H, 7, 0:DK], ACT.Copy).then_inc(n_rows, 1)
            with act.Fori(0, 4) as j:
                for q in range(2):
                    split_hi(act, 27 + q, j)
                    prep_hi(act, q, j, 1, 1, V_FFN0)

            def up_act(base, j, e, n, first=False):
                s = base % 2
                act.wait_ge(slab_done, base + 1 + 2 * j)
                nc.scalar.activation(halves(rbuf[:]), slab_ps(s), ACT.Relu).then_inc(ps_free[s], 1)
                split_hi(act, base + 2, j)
                if first:
                    rms(act, 1 + n)
                act.wait_ge(scaled, 32 * n + 1 + e)
                nc.scalar.activation(qbuf[:], tbuf[:], ACT.Square).then_inc(squared, 1)
                act.wait_ge(squared, 32 * n + 1 + e)
                return nc.scalar.activation

            def gains_out(k):
                s = k % 2
                act.wait_ge(gt_done, k + 1)
                if k >= 2:
                    act.wait_ge(v_done, k - 1)
                elif k == 0:
                    act.wait_ge(u_out, 16 * 4)
                nc.scalar.activation(GT[:, s].rearrange("p (r q) c -> p r (q c)", r=2), ps[:, GB[k]:GB[k] + 2, :],
                                     ACT.Copy).then_inc(gt_ready, 1)

            def ffn_act(l):
                up, down = I_FFN[l], I_FFN[l] + 8

                def tile_up(base, j, e, k, first=False):
                    up_act(base, j, e, l, first)
                    nc.scalar.activation(tile(hid_hi, k), qbuf[:], ACT.Copy).then_inc(hhi_done, 1)

                for e in range(2):
                    tile_up(up + e, 0, e, e, e == 0)
                with act.Fori(1, 4) as j:
                    for q in range(2):
                        tile_up(up + q, j, q + 2 * j, q + 2 * j)
                with act.Fori(0, FF - 1) as f:
                    with act.Fori(0, 4) as j:
                        for q in range(2):
                            split_hi(act, down + 2 + q, 8 * f + j)
                    with act.Fori(0, 4) as j:
                        for q in range(2):
                            tile_up(up + 16 + q, 8 * f + j, 8 + q + 8 * f + 2 * j, q + 2 * j)
                if l == 0:
                    for q in range(3):
                        split_hi(act, down + 50 + q, 0)
                    act.wait_ge(taps_done, 1)
                    nc.scalar.activation(h0[:].rearrange("p r b g -> p (r b g)"), ps[:, 4, :], ACT.Copy).then_inc(h0_act, 1)
                    for r in range(2):
                        nc.scalar.activation(ktap[:, 4 * r:4 * r + 4, PAD:TAPS], ps[:, 6 + r, :].rearrange("p (k c) -> p k c", k=4),
                                             ACT.Copy).then_inc(kt_act, 1)
                    for q in range(3, KT):
                        if q == 6:
                            gains_out(0)
                        split_hi(act, down + 50 + q, 0)
                    return
                with act.Fori(0, 3) as j:
                    for q in range(2):
                        split_hi(act, down + 50 + q, j)

            act.wait_ge(out_done, 16 * 11)
            for s in range(2):
                act.wait_ge(c_out[s], 16 * 3 * 4)
            ffn_act(0)

            def gelu(k):
                act.wait_ge(yn_in[k % 2], 16 * (k // 2 + 1))
                act.wait_ge(hid_ready, HID0[1] - KT + k)
                nc.scalar.activation(blocks(yv[:]), steps(yn[k % 2]), ACT.Gelu_apprx_tanh).then_inc(gel_done, 1)
                act.wait_ge(gel_done, k + 1)
                if k >= KT - 2:
                    act.wait_ge(sy_done, KT)
                nc.scalar.activation(hid_hi[:, k], yv[:], ACT.Copy).then_inc(hhi_done, 1)

            act.wait_ge(r2_pe, 1)
            nc.scalar.activation(R2[:], ps[:, 6, 0:COLS], ACT.Sqrt, bias=eps[:, 0:1], scale=1.0 / D).then_inc(r2_act, 1)
            for i in range(KT + 3):
                if i + 1 < KT:
                    gains_out(i + 1)
                if 0 <= i - 1 < KT:
                    k = i - 1
                    act.wait_ge(sy_done, k + 1)
                    nc.scalar.activation(U2[:, 8 * k:8 * k + 8, :].rearrange("p (q a) b -> p a q b", a=2),
                                         ps[:, 6:8, 0:4 * COLS].rearrange("p a (q b) -> p a q b", q=4),
                                         ACT.Copy).then_inc(yev_ready, 1)
                for k in GELUS.get(i, ()):
                    gelu(k)
            act.wait_ge(ssend_pe, 1)
            nc.scalar.activation(srow[:].rearrange("p a b -> p (a b)"), ps[:, 4, :], ACT.Copy)
            nc.scalar.activation(prow[:], ps[0:2 * GP, 5, 0:P], ACT.Copy).then_inc(ssend_rows, 1)
            with act.Fori(0, 4) as j:
                for q in range(2):
                    base = I_GLU + 2 * q
                    split_hi(act, base + 2, 2 * j)
                    act.wait_ge(slab_done, base + 1 + 4 * j)
                    act.wait_ge(ps_free[0], I_GLU // 2 + 1 + q + 2 * j)
                    nc.scalar.activation(halves(gbuf[:]), slab_ps(1), ACT.Tanh, scale=0.5).then_inc(ps_free[1], 1)
                    split_hi(act, base + 3, 2 * j)
                    prep_hi(act, q, j, 3, 2, V_FFN1)
            ffn_act(1)
            for k in range(KT):
                wait_x(act, 4, k)
                nc.scalar.activation(xf[:, k], x[:, k], ACT.Identity, scale=gain(V_FIN, k)).then_inc(xf_ready, 1)
            act.wait_ge(fin_pe, 1)
            nc.scalar.activation(fin[0:TS, 0:1], ps[0:TS, 4, 0:1], ACT.Sqrt, bias=eps[0:TS, 0:1], scale=1.0 / D)
            nc.scalar.activation(fin[:, 1:5], ps[:, 4, 2:10:2], ACT.Sqrt, bias=eps[:, 0:1], scale=1.0 / D).then_inc(fin_act, 1)
            act.wait_ge(fin_ready, 1)
            for i in range(5):
                n = TS if i == 0 else P
                act.wait_ge(yt_done, i + 1)
                nc.scalar.activation(finished[i][:, 0:512], ps[0:n, YB[i], :], ACT.Copy, scale=fin[0:n, i:i + 1]).then_inc(y_act, 1)

        @block.vector
        def _(dve):
            own = Steps(dve, dve_step)
            V = nc.vector
            lr, li, lrdt, lidt, mag, t6, t9, t19 = (lg[:, n, :] for n in (0, 1, 2, 3, 4, 6, 9, 19))
            dve.wait_ge(lam_act, 1)
            dtb = dt2[:, 1, :].unsqueeze(2).to_broadcast([GP, 2, SP])
            for r in range(2):
                last = V.tensor_tensor(lg[:, 2 + r, :].rearrange("a (b p) -> a b p", b=2),
                                       lg[:, r, :].rearrange("a (b p) -> a b p", b=2), dtb, ALU.mult)
            last.then_inc(lam_dve, 1)
            dve.wait_ge(lam_dve, 1)
            for r, shift in ((7, 0.0), (8, 0.25)):
                own.link(V.tensor_scalar(t6, lidt, 1.0 / (2 * np.pi), shift, ALU.mult, ALU.add))
                own.link(V.tensor_scalar(t6, t6, MAGIC, None, ALU.add))
                own.link(V.tensor_scalar(t6, t6, -MAGIC, None, ALU.add))
                own.link(V.scalar_tensor_tensor(lg[:, r, :], t6, -TWO_PI_HI, lidt, ALU.mult, ALU.add))
                own.link(V.scalar_tensor_tensor(lg[:, r, :], t6, -TWO_PI_LO, lg[:, r, :], ALU.mult, ALU.add))
            own.link(V.tensor_scalar(lg[:, 8, :], lg[:, 8, :], float(np.pi / 2), None, ALU.add))
            V.tensor_scalar(lg[:, 7:9, :], lg[:, 7:9, :], 3.1415925, -3.1415925, ALU.min, ALU.max).then_inc(lam_dve, 1)
            dve.wait_ge(vec_pe, 1)
            V.tensor_copy(vec[:].rearrange("p v k -> p (v k)"), ps[:, 4, 0:56]).then_inc(vec_ready, 1)
            dve.wait_ge(vec_pe, 2)
            V.tensor_copy(nT[:], ps[:, 7, 0:32]).then_inc(vec_ready, 1)
            for k in range(KT + 1):
                if k < KT:
                    r = 2 * (k % 2)
                    dve.wait_ge(xt_done, k + 1)
                    V.tensor_copy(x[:, k, TS:N], ps[:, r, :])
                    V.tensor_copy(x[:, k, 0:TS], ps[:, r + 1, 0:TS]).then_inc(x_ready, 1)
                if k:
                    prep_lo(dve, k - 1, 0, V_MIX0)
                if k in (3, KT):
                    split_lo(dve, 0 if k == 3 else 1, 0)
            def scale_in(base, j, t):
                s = base % 2
                dve.wait_ge(slab_done, base + 1 + 2 * j)
                V.tensor_tensor(halves(tile(qkvo, t)), slab_ps(s), halves(R[:]), ALU.mult).then_inc(ps_free[s], 1)

            inv_rms(dve, 0)
            scale_in(0, 0, 24)
            split_lo(dve, 2, 0)
            scale_in(1, 0, 0)
            split_lo(dve, 3, 0)
            scale_in(2, 0, 1)
            split_lo(dve, 4, 0)
            def pair_in(j):
                for q in range(2):
                    scale_in(3 + q, j, 2 + q + 2 * j)
                    split_lo(dve, 5 + q, j)

            dve.wait_ge(gate_pe, 1)
            dve.wait_ge(gate_in, 48)
            V.tensor_scalar(halves(gw[:, LI, :]), ps[0:8, 4:6, 0:HN], gs[:, BI:BI + 1], None, ALU.add)
            dve.wait_ge(gate_act, 1)
            own.link(V.tensor_scalar(halves(gw[:, LF, :]), ps[0:8, 6:8, 0:HN], gs[:, BF:BF + 1], 0.0, ALU.add, ALU.min))
            own.link(V.tensor_tensor(gw[:, LF, :], gw[:, LF, :], gw[:, GT1, :], ALU.subtract))
            dve.wait_ge(am_ready, 1)
            own.link(V.tensor_tensor_scan(gw[:, BC, :], gw[:, AM, :], gw[:, LF, :], 0.0, ALU.mult, ALU.add))
            first = slice(0, TS + 1, T)
            own.link(V.tensor_tensor(gw[:, GT2, 0:9], gw[:, LF, first], gs[:, M0:M0 + 9], ALU.add))
            own.link(V.tensor_copy(gw[:, GT1, :], gw[:, LI, :]))
            own.link(V.tensor_tensor(gw[:, GT1, first], gw[:, GT1, first], gw[:, GT2, 0:9], ALU.max))
            own.link(V.memset(gw[:, LF, first], -1e30))
            own.link(V.tensor_tensor_scan(gw[:, MM, :], gw[:, LF, :], gw[:, GT1, :], 0.0, ALU.add, ALU.max))
            scale_in(3, 0, 2)
            split_lo(dve, 5, 0)
            u = qkvo[0:8, 24, :]
            dve.wait_ge(q4_clear, 1)
            V.tensor_copy(gs[:, MPT:MPT + B], gw[:, MM, T - 1:TS:T])
            V.tensor_copy(gs[:, MPT + B:MPT + B + 1], gw[:, MM, N - 1:N])
            own.link(V.tensor_tensor(u, gw[:, BC, :], gw[:, MM, :], ALU.subtract))
            own.link(V.tensor_tensor(Q4[0:8, :], gw[:, LI, :], gw[:, BC, :], ALU.subtract))
            own.link(V.tensor_tensor(gw[:, GT2, 0:TS].rearrange("h (b t) -> h b t", b=B),
                                     Q4[0:8, 0:TS].rearrange("h (b t) -> h b t", b=B),
                                     u[:, T - 1:TS:T].unsqueeze(2).to_broadcast([8, B, T]), ALU.add))
            own.link(V.tensor_scalar(gw[:, GT2, TS:N], Q4[0:8, TS:N], u[:, N - 1:N], None, ALU.add))
            V.tensor_copy(Q4[32:40, :], gw[:, GT2, :])
            V.tensor_scalar(Q4[64:72, :], gw[:, MM, :], -1.0, None, ALU.mult)
            own.link(V.tensor_tensor(gw[:, GT1, 0:TS].rearrange("h (b t) -> h b t", b=B),
                                     u[:, 0:TS].rearrange("h (b t) -> h b t", b=B),
                                     gs[:, M0:M0 + B].unsqueeze(2).to_broadcast([8, B, T]), ALU.add))
            V.tensor_tensor(gs[:, DEC:DEC + B], u[:, T - 1:TS:T], gs[:, M0:M0 + B], ALU.add).then_inc(m_ready, 1)
            V.tensor_copy(Q4[96:104, 0:TS], gw[:, GT1, 0:TS]).then_inc(q4_ready, 1)

            def c_columns(ri):
                dve.wait_ge(craw_pe, ri + 1)
                for g2 in range(2):
                    hf = slice(g2 * SP, (g2 + 1) * SP)
                    last = V.tensor_copy(cT[hf, ri], ps[hf, 6:8, :].rearrange("p b (q g c) -> p (b q) g c", g=2, c=GC)[:, :, g2, :])
                last.then_inc(craw_ready, 1)

            scale_in(4, 0, 3)
            split_lo(dve, 6, 0)
            dve.wait_ge(lam_act, 3)
            sin, cos, a_re, a_im = (lg[:, n, :] for n in (10, 11, 12, 13))
            V.tensor_tensor(a_re, mag, cos, ALU.mult)
            V.tensor_tensor(t6, lr, lr, ALU.mult)
            V.tensor_tensor(t9, li, li, ALU.mult)
            own.link(V.tensor_tensor(a_im, mag, sin, ALU.mult))
            own.link(V.tensor_tensor(t6, t6, t9, ALU.add))
            own.link(V.reciprocal(lg[:, 5, :], t6))
            V.tensor_scalar(t19, a_re, -1.0, None, ALU.add)
            own.link(V.tensor_tensor(t9, a_im, li, ALU.mult))
            own.link(V.tensor_tensor(t6, t19, lr, ALU.mult))
            own.link(V.tensor_tensor(t6, t6, t9, ALU.add))
            own.link(V.tensor_tensor(lg[:, 14, :], t6, lg[:, 5, :], ALU.mult))
            V.tensor_tensor(t6, a_im, lr, ALU.mult)
            own.link(V.tensor_tensor(t9, t19, li, ALU.mult))
            own.link(V.tensor_tensor(t6, t6, t9, ALU.subtract))
            own.link(V.tensor_tensor(lg[:, 15, :], t6, lg[:, 5, :], ALU.mult))
            c, s = cos, sin
            for n in range(3):
                own.link(V.tensor_tensor(t6, c, c, ALU.mult))
                own.link(V.tensor_tensor(t9, s, s, ALU.mult))
                own.link(V.scalar_tensor_tensor(t19, c, 2.0, s, ALU.mult, ALU.mult))
                own.link(V.tensor_tensor(lg[:, 17, :], t6, t9, ALU.subtract))
                last = V.tensor_copy(lg[:, 18, :], t19)
                if n < 2:
                    own.link(last)
                c, s = lg[:, 17, :], lg[:, 18, :]
            last.then_inc(lam_dve, 1)
            pair_in(1)
            dve.wait_ge(lam_pe, 1)
            V.tensor_copy(s5s[:].rearrange("p v k -> p (v k)"), ps[:, 5, 0:224]).then_inc(craw_ready, 1)
            c_columns(0)
            pair_in(2)
            c_columns(1)
            dve.wait_ge(gate_act, 2)
            dve.wait_ge(const_done, 2)
            V.tensor_tensor(gw[:, LF, 0:64].rearrange("k (h b) -> k h b", h=H),
                            ident[0:8, 0:8].unsqueeze(2).to_broadcast([8, H, B]),
                            gs[:, DEC:DEC + B].unsqueeze(1).to_broadcast([8, H, B]), ALU.mult).then_inc(dec_rhs, 1)
            with dve.Fori(3, 10) as j:
                pair_in(j)
            pair_in(10)
            for i in range(1, 12, 2):
                dve.wait_ge(kv_done, i + 1)
                r = 2 * (i % 4)
                if i < 4:
                    V.tensor_copy(Ktok[:, 1:5, i, :], ps[:, r, :].rearrange("p (i c) -> p i c", i=NB))
                    V.tensor_copy(Ktok[0:TS, 0, i, :], ps[0:TS, r + 1, 0:P]).then_inc(kv_dve, 1)
                else:
                    V.tensor_copy(Vtok[:, 1:5, i - 4, 0:DV], ps[:, r, :].rearrange("p (i c) -> p i c", i=NB))
                    V.tensor_copy(Vtok[0:TS, 0, i - 4, 0:DV], ps[0:TS, r + 1, 0:P]).then_inc(kv_dve, 1)
            dve.wait_ge(ex_ready, 2)
            dve.wait_ge(att_const, 1)
            own.link(V.memset(st5[:, 6, :], -0.5))

            def weights(h):
                e = E[:, h % 2]
                dve.wait_ge(exp_done, h + 1)
                dve.wait_ge(s_done, h + 1)
                flat = ps[:].rearrange("p b c -> p (b c)")
                V.scalar_tensor_tensor(e[:, 0:1280], flat[:, 512:1792], DK ** -0.5, e[:, 0:1280], ALU.mult, ALU.mult)
                V.scalar_tensor_tensor(e[0:TS, 1280:1344], flat[0:TS, 1792:1856], DK ** -0.5, Es[:, h * TS:(h + 1) * TS],
                                       ALU.mult, ALU.mult).then_inc(p_done, 1)

            def decayed(h, b4, new):
                c = Cst[:, h % 2, b4, :]
                return V.scalar_tensor_tensor(c, c, dcy[:, h, b4:b4 + 1], new, ALU.mult, ALU.add)

            def states_a(h):
                dve.wait_ge(upa_done, h + 1)
                for b4 in range(3):
                    last = decayed(h, b4, ps[:, 7, b4 * E1:(b4 + 1) * E1])
                own.link(last)
                dve.wait_ge(cb_done, h + 1)
                V.tensor_copy(nN[:, :, h], Cst[:, h % 2, :, DV]).then_inc(c_new, 1)

            def states_b(h):
                dve.wait_ge(upb_done, h + 1)
                if h >= 2:
                    dve.wait_ge(c_out[h % 2], 16 * 3 * (h // 2))
                V.tensor_copy(CP[:, h % 2, :], ps[0:DK, 4, E1:E1 + DV])
                V.tensor_copy(nP[:, h:h + 1], ps[0:DK, 4, E1 + DV:2 * E1])
                decayed(h, 3, ps[:, 4, 0:E1]).then_inc(cb_done, 1)

            def gated(h):
                dve.wait_ge(osig_ready, h + 1)
                dve.wait_ge(ht_done, h + 1)
                o = qkvo[:, 16 + h]
                V.scalar_tensor_tensor(o[:, TS:N], ps[:, 6, :], gain(V_HEAD, h), o[:, TS:N], ALU.mult, ALU.mult)
                V.scalar_tensor_tensor(o[:, 0:TS], ps[:, 7, 448:512], gain(V_HEAD, h), o[:, 0:TS], ALU.mult,
                                       ALU.mult).then_inc(hf_ready, 1)

            def gated_lo(h):
                dve.wait_ge(hhi_done, h + 1)
                V.tensor_tensor(hid_lo[:, h], qkvo[:, 16 + h], hid_hi[:, h].bitcast(F32), ALU.subtract).then_inc(hid_ready, 1)

            dve.wait_ge(us_done, 1)
            V.tensor_tensor(Es.rearrange("s (h t) -> s h t", h=H), ps[0:TS, 7, :].rearrange("s (h t) -> s h t", h=H),
                            TK[0:TS, 0, 0:H].unsqueeze(2).to_broadcast([TS, H, TS]), ALU.add).then_inc(us_arg, 1)
            dve.wait_ge(us_arg, 1)
            V.tensor_scalar(Es, Es, 0.0, None, ALU.min).then_inc(us_arg, 1)
            dve.wait_ge(es_ready, 1)
            weights(0)
            def head_norm(h):
                own.link(V.scalar_tensor_tensor(st5[:, 0, :], OT[:, :, DV], -1.0, OT[:, :, DV], ALU.mult, ALU.max))
                own.link(V.tensor_tensor(st5[:, 0, :], st5[:, 0, :], EX[:, :, 32 + h], ALU.max))
                own.link(V.reciprocal(st5[:, 1, :], st5[:, 0, :]))
                own.link(V.tensor_tensor(st5[:, 3, :], st5[:, 1, :], st5[:, 1, :], ALU.mult))
                dve.wait_ge(ssq_done, h + 1)
                own.link(V.tensor_tensor(st5[:, 3, :], st5[:, 3, :], st5[:, 2, :], ALU.mult))
                V.tensor_scalar(st5[:, 4, :], st5[:, 3, :], 1.0 / DV, EPS, ALU.mult, ALU.add).then_inc(ms_ready, 1)

            def normed(h):
                dve.wait_ge(rstd_ready, h + 1)
                own.link(V.tensor_tensor(st5[:, 7, :], st5[:, 5, :], st5[:, 1, :], ALU.mult))
                V.tensor_tensor(Htok[:], OT[:, :, 0:DV], st5[:, 7, :].unsqueeze(2).to_broadcast([P, 5, DV]),
                                ALU.mult).then_inc(htok_ready, 1)

            for h in range(H + 1):
                if h:
                    states_b(h - 1)
                    head_norm(h - 1)
                    states_a(h - 1)
                if h:
                    normed(h - 1)
                if h + 1 < H:
                    weights(h + 1)
                if h:
                    gated(h - 1)
                if h < H:
                    dve.wait_ge(ot_act, h + 1)
                    V.tensor_tensor(OT[0:TS, 0, :], ps[0:TS, 5, E1:2 * E1], Is[:], ALU.add).then_inc(ot_ready, 1)
                    dve.wait_ge(ot_ready, h + 1)
                if h:
                    gated_lo(h - 1)

            def add_down(base, j, m):
                s = base % 2
                dve.wait_ge(slab_done, base + 1 + 2 * j)
                V.tensor_tensor(halves(tile(x, m)), halves(tile(x, m)), slab_ps(s), ALU.add).then_inc(ps_free[s], 1)

            with dve.Fori(0, 4) as j:
                for q in range(2):
                    add_down(25 + q, j, 2 * j + q)
                    split_lo(dve, 27 + q, j)
                    prep_lo(dve, 2 * j + q, 1, V_FFN0)

            def ffn_dve(l):
                up, down = I_FFN[l], I_FFN[l] + 8

                def tile_up(base, j, e, k, first=False):
                    s = base % 2
                    if first:
                        split_lo(dve, base + 2, j)
                        inv_rms(dve, 1 + l)
                    dve.wait_ge(ps_free[s], base // 2 + 1 + j)
                    V.tensor_tensor(tbuf[:], rbuf[:], R[:], ALU.mult).then_inc(scaled, 1)
                    if not first:
                        split_lo(dve, base + 2, j)
                    dve.wait_ge(hhi_done, HID0[l] + 1 + e)
                    V.tensor_tensor(tile(hid_lo, k), qbuf[:], tile(hid_hi, k).bitcast(F32),
                                    ALU.subtract).then_inc(hid_ready, 1)

                for e in range(2):
                    tile_up(up + e, 0, e, e, e == 0)
                with dve.Fori(1, 4) as j:
                    for q in range(2):
                        tile_up(up + q, j, q + 2 * j, q + 2 * j)
                with dve.Fori(0, FF - 1) as f:
                    with dve.Fori(0, 4) as j:
                        for q in range(2):
                            add_down(down + q, 8 * f + j, 2 * j + q)
                            split_lo(dve, down + 2 + q, 8 * f + j)
                    with dve.Fori(0, 4) as j:
                        for q in range(2):
                            tile_up(up + 16 + q, 8 * f + j, 8 + q + 8 * f + 2 * j, q + 2 * j)
                if l == 0:
                    for k in range(KT):
                        add_down(down + 48 + k, 0, k)
                        wait_x(dve, 2, k)
                        if k == KT - 1:
                            last_squares(dve, 2)
                        if k == 0:
                            dve.wait_ge(slab_done, down + 48)
                        V.tensor_scalar(steps(unat[:, k]), blocks(x[:, k]), gain(V_MIX1, k), None, ALU.mult).then_inc(u_ready, 1)
                        split_lo(dve, down + 50 + k, 0)
                    return
                with dve.Fori(0, 3) as j:
                    for q in range(2):
                        add_down(down + 48 + q, j, 2 * j + q)
                        split_lo(dve, down + 50 + q, j)
                for q in range(2):
                    add_down(down + 54 + q, 0, 6 + q)

            ffn_dve(0)
            dve.wait_ge(r2_act, 1)
            V.reciprocal(R2[:], R2[:]).then_inc(r2_ready, 1)
            dve.wait_ge(r2_ready, 1)

            def normalised(k):
                dve.wait_ge(u2_in[k // 4], 16 * T)
                u = U2[:, 8 * k:8 * k + 8, :]
                V.tensor_tensor(u, u, R2[:].unsqueeze(1).to_broadcast([P, 8, COLS]), ALU.mult).then_inc(un_ready, 1)

            normalised(0)
            normalised(1)

            def states(k):
                g, s = slice(4 * k, 4 * k + 4), k % 2
                c, sn = EC[:, g], ES[:, g]
                vr, vi = (ps[:, 4 + ri, 0:4 * COLS].rearrange("p (q c) -> p q c", q=4)[:, :, B:COLS] for ri in range(2))
                v0 = ps[:, 4:6, 0:4 * COLS].rearrange("p r (q c) -> p r q c", q=4)[:, :, :, 0:B]
                V.tensor_copy(rho[:, :, 1:SP], s5s[:, MAG8, g].unsqueeze(2).to_broadcast([P, 4, SP - 1]))
                dve.wait_ge(v_done, k + 1)
                V.tensor_tensor(rot[:, 0], vr, c, ALU.mult)
                V.tensor_tensor(rot[:, 1], vi, sn, ALU.mult)
                V.tensor_tensor(rot[:, 2], vi, c, ALU.mult)
                V.tensor_tensor(rot[:, 3], vr, sn, ALU.mult)
                if k == 0:
                    dve.wait_ge(u_out, 16 * KT)
                own.link(V.tensor_copy(hN[:, :, :, g].rearrange("p r b g -> p r g b"), v0))
                V.tensor_tensor(rot[:, 0], rot[:, 0], rot[:, 1], ALU.add)
                V.tensor_tensor(rot[:, 2], rot[:, 2], rot[:, 3], ALU.subtract).then_inc(h_ready, 1)
                dve.wait_ge(h_ready, k + 1)
                flat = lambda ap: ap.rearrange("p q c -> p (q c)")
                V.tensor_tensor_scan(flat(rot[:, 1]), flat(rho[:]), flat(rot[:, 0]), 0.0, ALU.mult, ALU.add)
                own.link(V.tensor_tensor_scan(flat(rot[:, 3]), flat(rho[:]), flat(rot[:, 2]), 0.0, ALU.mult, ALU.add))
                V.tensor_tensor(rot[:, 0], rot[:, 1], c, ALU.mult)
                V.tensor_tensor(rot[:, 2], rot[:, 3], sn, ALU.mult)
                V.tensor_tensor(rot[:, 1], rot[:, 1], sn, ALU.mult)
                own.link(V.tensor_tensor(rot[:, 3], rot[:, 3], c, ALU.mult))
                if k >= 2:
                    dve.wait_ge(sy_done, k - 1)
                V.tensor_tensor(Hst[:, s, 0, :, B + 1:], rot[:, 0], rot[:, 2], ALU.subtract)
                V.tensor_tensor(Hst[:, s, 1, :, B + 1:], rot[:, 1], rot[:, 3], ALU.add)
                own.link(V.tensor_copy(Hst[:, s, :, :, 0:B], h0[:, :, :, g].rearrange("p r b g -> p r g b")))
                V.tensor_copy(hP[:, :, g], Hst[:, s, :, :, COLS]).then_inc(hst_ready, 1)

            def gelu_lo(k):
                dve.wait_ge(hhi_done, HID0[1] - KT + 1 + k)
                V.tensor_tensor(hid_lo[:, k], yv[:], hid_hi[:, k].bitcast(F32), ALU.subtract).then_inc(hid_ready, 1)

            dve.wait_ge(s5_set, 1)
            for i in range(KT + 3):
                if i < KT:
                    states(i)
                if i + 2 < KT:
                    normalised(i + 2)
                for k in GELU_LOS.get(i, ()):
                    gelu_lo(k)
            with dve.Fori(0, 4) as j:
                for q in range(2):
                    base = I_GLU + 2 * q
                    split_lo(dve, base + 2, 2 * j)
                    dve.wait_ge(ps_free[1], base // 2 + 1 + 2 * j)
                    V.tensor_scalar(sbuf[:], gbuf[:], 1.0, 0.5, ALU.add, ALU.mult).then_inc(sig_done, 1)
                    split_lo(dve, base + 3, 2 * j)
                    dve.wait_ge(sig_done, 1 + q + 2 * j)
                    dve.wait_ge(slab_done, base + 2 + 4 * j)
                    V.tensor_tensor(halves(tb2[:]), slab_ps(0), halves(sbuf[:]), ALU.mult).then_inc(glu_done, 1)
                    dve.wait_ge(glu_done, 1 + q + 2 * j)
                    k = q + 2 * j
                    V.tensor_tensor(tile(x, k), tile(x, k), tb2[:], ALU.add).then_inc(ps_free[0], 1)
                    prep_lo(dve, k, 2, V_FFN1)
            ffn_dve(1)
            last_squares(dve, 4)
            dve.wait_ge(fin_act, 1)
            V.reciprocal(fin[0:TS, 0:1], fin[0:TS, 0:1])
            V.reciprocal(fin[:, 1:5], fin[:, 1:5]).then_inc(fin_ready, 1)
            dve.wait_ge(fin_ready, 1)
            for i in range(5):
                n = TS if i == 0 else P
                dve.wait_ge(yt_done, i + 1)
                V.tensor_scalar(finished[i][:, 512:1024], ps[0:n, YB[i] + 1, :], fin[0:n, i:i + 1], None, ALU.mult).then_inc(y_dve, 1)

        @block.tensor
        def _(pe):
            pe.wait_ge(const_done, 1)
            pe.wait_ge(vec_in, 16 * 5)
            nc.tensor.transpose(ps[:, 4, 0:56], vrow[:], ident[0:56, 0:56]).then_inc(vec_pe, 1)
            pe.wait_ge(nrow_in, 16 * 8)
            nc.tensor.transpose(ps[:, 7, 0:32], nrow[:], ident[0:32, 0:32]).then_inc(vec_pe, 1)
            pe.wait_ge(x_in, 16 * 5)
            for k in range(KT):
                r = 2 * (k % 2)
                if k >= 2:
                    pe.wait_ge(x_ready, k - 1)
                for i in range(NB):
                    nc.tensor.transpose(ps[:, r, i * P:(i + 1) * P], xtok[:, 1 + i, k * P:(k + 1) * P], ident[:])
                nc.tensor.transpose(ps[:, r + 1, 0:TS], xtok[0:TS, 0, k * P:(k + 1) * P],
                                    ident[0:TS, 0:TS]).then_inc(xt_done, 1)
            pe.wait_ge(x_ready, KT - 1)
            pe.wait_ge(const_done, 2)
            xg, hid = (xg_hi, xg_lo), (hid_hi, hid_lo)
            product(pe, 0, 0, xg, (xg_ready, 0))
            pe.wait_ge(vec_ready, 1)
            stats(pe, 0)
            pe.wait_ge(x_ready, KT)
            product(pe, 1, 0, xg)
            product(pe, 2, 0, xg)
            pe.wait_ge(vec_ready, 2)
            pe.wait_ge(R_ready, 1)
            for g in range(2):
                for c in range(2):
                    last = nc.tensor.matmul(ps[0:8, 4 + 2 * g + c, 0:HN], ident[:, GATE_ROW + 8 * g:GATE_ROW + 8 * g + 8],
                                            qkvo[:, 24, c * HN:(c + 1) * HN], start=True, stop=True)
            last.then_inc(gate_pe, 1)

            def pair_in(j):
                for q in range(2):
                    product(pe, 3 + q, j, xg)

            def c_turn(ri):
                for k in range(KT):
                    last = nc.tensor.transpose(ps[:, 6 + k // 4, k % 4 * P:(k % 4 + 1) * P],
                                               craw[:, ri, k].rearrange("p a b -> p (a b)"), ident[:])
                last.then_inc(craw_pe, 1)

            pair_in(0)
            pair_in(1)
            pe.wait_ge(lam_dve, 3)
            pe.wait_ge(gate_act, 1)
            pe.wait_ge(m_ready, 1)
            for v in range(7):
                last = nc.tensor.transpose(ps[:, 5, v * GP:(v + 1) * GP], lg[:, 12 + v, :], ident[0:GP, 0:GP])
            last.then_inc(lam_pe, 1)
            pe.wait_ge(craw_in, 64)
            c_turn(0)
            pair_in(2)
            pe.wait_ge(craw_ready, 2)
            c_turn(1)
            with pe.Fori(3, 10) as j:
                pair_in(j)
            pe.wait_ge(q4_ready, 1)
            pe.wait_ge(craw_ready, 3)
            nc.tensor.transpose(ps[0:TS, 4, 0:P], Q4[:, 0:TS], ident[:])
            for i in range(NB):
                nc.tensor.transpose(ps[:, 5, i * P:(i + 1) * P], Q4[:, TS + i * P:TS + (i + 1) * P], ident[:])
            pe.wait_ge(dec_rhs, 1)
            nc.tensor.matmul(ps[:, 6, 0:64], ones[0:8, :], gw[:, LF, 0:64], start=True, stop=True).then_inc(tk_pe, 1)
            pair_in(10)
            pe.wait_ge(ps_free[0], 13)
            pe.wait_ge(ps_free[1], 12)
            pe.wait_ge(ex_ready, 2)
            for i in range(12):
                r = 2 * (i % 4)
                if i >= 4:
                    if i % 2:
                        pe.wait_ge(kv_dve, i // 2 - 1)
                    else:
                        pe.wait_ge(kv_act, i // 2 - 1)
                for n in range(NB):
                    nc.tensor.transpose(ps[:, r, n * P:(n + 1) * P], qkvo[:, 4 + i, TS + n * P:TS + (n + 1) * P], ident[:])
                nc.tensor.transpose(ps[0:TS, r + 1, 0:P], qkvo[:, 4 + i, 0:TS], ident[:]).then_inc(kv_done, 1)
            pe.wait_ge(kv_act, 6)
            pe.wait_ge(kv_dve, 6)
            pe.wait_ge(att_const, 2)

            def spread(h):
                if h:
                    pe.wait_ge(exp_done, h)
                nc.tensor.matmul(ps[:, 0, :], SEL[:, h, :], qkvo[0:8, 24, TS:N], start=True, stop=True).then_inc(u_done, 1)

            def scores(h):
                if h:
                    pe.wait_ge(p_done, h)
                hp = h % 2 * DK
                q, k = qkvo[hp:hp + DK, h // 2], qkvo[hp:hp + DK, 4 + h // 2]
                for j, (b, c) in enumerate(((1, 0), (2, 0), (3, 0), (2, 384))):
                    w = L - j * P
                    nc.tensor.matmul(ps[:, b, c:c + w], k[:, TS + j * P:TS + (j + 1) * P], q[:, TS + j * P:N],
                                     start=True, stop=True)
                nc.tensor.matmul(ps[0:TS, 3, 256:320], k[:, 0:TS], q[:, 0:TS], start=True, stop=True).then_inc(s_done, 1)

            def heads_out(h):
                pe.wait_ge(htok_ready, h + 1)
                pe.wait_ge(c_new, h + 1)
                if h:
                    pe.wait_ge(hf_ready, h)
                for i in range(NB):
                    nc.tensor.transpose(ps[:, 6, i * P:(i + 1) * P], Htok[:, 1 + i, :], ident[:])
                nc.tensor.transpose(ps[:, 7, 448:512], Htok[0:TS, 0, :], ident[0:TS, 0:TS]).then_inc(ht_done, 1)

            def sums(h):
                e = E[:, h % 2]
                pe.wait_ge(p_masked, h + 1)
                pe.wait_ge(qblk_ready, h + 1)
                pe.wait_ge(ncol_ready, h + 1)
                if h:
                    pe.wait_ge(ot_ready, h)
                    pe.wait_ge(cb_done, h)
                for i in range(NB):
                    o = ps[:, 4, i * E1:(i + 1) * E1] if i < 3 else ps[:, 5, 0:E1]
                    for j in range(i + 1):
                        c = OFF[j] + (i - j) * P
                        nc.tensor.matmul(o, e[:, c:c + P], Vtok[:, 1 + j, h, :], start=(j == 0), stop=(j == i))
                nc.tensor.matmul(ps[0:TS, 5, E1:2 * E1], e[0:TS, 1280:1344], Vtok[0:TS, 0, h, :], start=True, stop=True)
                for b4 in range(4):
                    last = nc.tensor.matmul(ps[0:TS, 5, 2 * E1:3 * E1], Qblk[:, b4 * TS:(b4 + 1) * TS], Cst[:, h % 2, b4, :],
                                            start=(b4 == 0), stop=(b4 == 3))
                last.then_inc(pv_done, 1)

            def key_values(h, b4, out):
                return nc.tensor.matmul(out, Kblk[:, h % 2, 2 * b4:2 * b4 + 2, :].rearrange("s b d -> s (b d)"),
                                        Vtok[0:TS, 0, h, :], start=True, stop=True)

            def updates_a(h):
                pe.wait_ge(kws_ready, h + 1)
                if h:
                    pe.wait_ge(hf_ready, h)
                for b4 in range(3):
                    last = key_values(h, b4, ps[:, 7, b4 * E1:(b4 + 1) * E1])
                last.then_inc(upa_done, 1)

            def updates_b(h):
                pe.wait_ge(ot_act, h + 1)
                pe.wait_ge(kws_ready, h + 1)
                key_values(h, 3, ps[:, 4, 0:E1])
                for j in range(NB):
                    last = nc.tensor.matmul(ps[0:DK, 4, E1:2 * E1], Kws[:, h % 2, 1 + j, :], Vtok[:, 1 + j, h, :],
                                            start=(j == 0), stop=(j == NB - 1))
                last.then_inc(upb_done, 1)

            for h in range(H):
                last = nc.tensor.matmul(ps[0:TS, 7, h * TS:(h + 1) * TS], SEL[:, h, 0:TS], qkvo[0:8, 24, 0:TS],
                                        start=True, stop=True)
            last.then_inc(us_done, 1)
            spread(0)
            scores(0)
            spread(1)
            pe.wait_ge(us_arg, 1)
            for h in range(H + 1):
                if h:
                    updates_b(h - 1)
                if h + 1 < H:
                    scores(h + 1)
                if h:
                    updates_a(h - 1)
                if h < H:
                    sums(h)
                else:
                    pe.wait_ge(p_done, H)
                    product(pe, I_OUT, 0, hid, (hid_ready, 0), range(KT - 1))
                if h:
                    heads_out(h - 1)
                if h + 2 < H:
                    spread(h + 2)
            product(pe, I_OUT + 1, 0, hid, None, range(KT - 1))
            pe.wait_ge(c_new, H)
            pe.wait_ge(hf_ready, H)
            nc.tensor.transpose(ps[0:32, 6, 256:384], nN[:].rearrange("p b h -> p (b h)"), ident[:])
            nc.tensor.transpose(ps[0:H, 7, 0:DK], nP[:], ident[0:DK, 0:DK]).then_inc(n_pe, 1)
            for i in range(2):
                product(pe, I_OUT + i, 0, hid, (hid_ready, 0), (KT - 1,))
            with pe.Fori(0, 3) as j:
                for q in range(2):
                    product(pe, 27 + q, j, hid)

            def taps():
                pe.wait_ge(bb_done, 1)
                for k in range(KT):
                    for q in range(4):
                        g = 4 * k + q
                        for ri in range(2):
                            last = nc.tensor.matmul(ps[32 * q:32 * q + 32, 6 + k // 4, k % 4 * P:(k % 4 + 1) * P],
                                                    bblk[:, ri, g].rearrange("p a c -> p (a c)"),
                                                    CA[:, ri, g, 0:T, :].rearrange("p j c -> p (j c)"),
                                                    start=(ri == 0), stop=(ri == 1))
                pe.wait_ge(st5_in, 64)
                for i in range(4):
                    last = nc.tensor.transpose(ps[:, 4, i * P:(i + 1) * P], srow[:, i, :], ident[:])
                last.then_inc(taps_done, 1)

            def gains_turn(k):
                pe.wait_ge(gs_ready, k + 1)
                if k == 0:
                    pe.wait_ge(kt_act, 2)
                elif k >= 3:
                    pe.wait_ge(gt_ready, k - 1)
                for ri in range(2):
                    for q in range(4):
                        last = nc.tensor.transpose(ps[:, GB[k] + ri, q * P:(q + 1) * P], gains_by[k % 2][:, ri, q, :], ident[:])
                last.then_inc(gt_done, 1)

            def ffn_pe(l):
                up, down = I_FFN[l], I_FFN[l] + 8
                product(pe, up, 0, xg, (xg_ready, KT * (1 + l)))
                stats(pe, 1 + 2 * l)
                product(pe, up + 1, 0, xg)
                with pe.Fori(0, 3) as j:
                    for q in range(2):
                        product(pe, up + 2 + q, j, xg)
                with pe.Fori(0, FF - 1) as f:
                    product(pe, down, 8 * f, hid, (hid_ready, HID0[l] + 8 * f))
                    product(pe, down + 1, 8 * f, hid)
                    with pe.Fori(0, 3) as j:
                        for q in range(2):
                            product(pe, down + 2 + q, 8 * f + j, hid)
                    with pe.Fori(0, 4) as j:
                        for q in range(2):
                            product(pe, up + 16 + q, 8 * f + j, xg)
                product(pe, down + 48, 0, hid, (hid_ready, HID0[l] + 24))
                for i in range(1, KT):
                    if l == 0 and i == 3:
                        taps()
                    if l == 0 and i == 4:
                        gains_turn(0)
                    product(pe, down + 48 + i, 0, hid)

            ffn_pe(0)

            def block_sums(k):
                s = k % 2
                pe.wait_ge(gt_ready, k + 1)
                if k:
                    pe.wait_ge(h_ready, k)
                pe.wait_ge(un_ready, k + 1)
                for q in range(4):
                    for g2 in range(2):
                        hf = slice(g2 * SP, (g2 + 1) * SP)
                        for ri in range(2):
                            last = nc.tensor.matmul(ps[hf, 4 + ri, q * COLS:(q + 1) * COLS], GT[:, s, 4 * ri + q, hf],
                                                    U2[:, 8 * k + 2 * q + g2, :], start=True, stop=True)
                last.then_inc(v_done, 1)

            def answers(k):
                s = k % 2
                pe.wait_ge(hst_ready, k + 1)
                if k < KT - 2:
                    pe.wait_ge(mt_in[s], 16 * T * (k // 2 + 1))
                else:
                    pe.wait_ge(late_in[s], 16 * T)
                if k:
                    pe.wait_ge(yev_ready, k)
                for q in range(4):
                    for g2 in range(2):
                        g8, st = 2 * q + g2, slice(g2 * SP, (g2 + 1) * SP)
                        for hf in range(2):
                            o = ps[hf * 64:(hf + 1) * 64, 6 + g2, q * COLS:(q + 1) * COLS]
                            nc.tensor.matmul(o, taps_of[k][:, g8, hf * 64:(hf + 1) * 64], U2[:, 8 * k + g8, :], start=True, stop=False)
                            for ri in range(2):
                                last = nc.tensor.matmul(
                                    o, CA[st, ri, 4 * k + q, 1 + 4 * hf:5 + 4 * hf, :].rearrange("p j c -> p (j c)"),
                                    Hst[st, s, ri, q, 0:COLS], start=False, stop=(ri == 1))
                last.then_inc(sy_done, 1)

            pe.wait_ge(ps_free[0], I_GLU // 2 + 1)
            pe.wait_ge(ps_free[1], I_GLU // 2)
            pe.wait_ge(acc_done, ACC0[3])
            pe.wait_ge(sq7_done, 1)
            pe.wait_ge(row_sel, 1)
            pe.wait_ge(gt_ready, 1)
            for i in range(T):
                hf, c = slice(i // 4 * 64, i // 4 * 64 + 64), (7 - i % 4) * GC
                for a in (acc, R):
                    last = nc.tensor.matmul(ps[hf, 6, 0:COLS], rowsel[:, c:c + 64], a[:, T - 1 - i::T],
                                            start=(i % 4 == 0 and a is acc), stop=(i % 4 == 3 and a is R))
            last.then_inc(r2_pe, 1)
            gains_turn(1)
            pe.wait_ge(h0_act, 1)
            pe.wait_ge(r2_act, 1)
            for i in range(KT + 1):
                if 0 < i < KT - 1:
                    gains_turn(i + 1)
                if i < KT:
                    block_sums(i)
                if i:
                    answers(i - 1)
            pe.wait_ge(pool_pre, 1)
            for i in range(4):
                nc.tensor.transpose(ps[:, 4, i * P:(i + 1) * P], hN[:, i // 2].rearrange("p b g -> p (b g)")[:, i % 2 * P:(i % 2 + 1) * P], ident[:])
            nc.tensor.transpose(ps[0:2 * GP, 5, 0:P], hP[:].rearrange("p r g -> p (r g)"), ident[:]).then_inc(ssend_pe, 1)
            for ks in (range(KT - 1), (KT - 1,)):
                for i in range(2):
                    product(pe, I_GLU + i, 0, hid, (hid_ready, HID0[1] - KT), ks)
            with pe.Fori(0, 7) as j:
                for q in range(2):
                    product(pe, I_GLU + 2 + q, j, hid)
            pe.wait_ge(ssend_rows, 1)
            ffn_pe(1)
            pe.wait_ge(acc_done, ACC0[5])
            pe.wait_ge(sq7_done, 2)
            for c in range(0, N, 64):
                hf, i = (0, 0) if c == 0 else ((c - TS) // 64 % 2, 1 + (c - TS) // P)
                for a in (acc, R):
                    last = nc.tensor.matmul(ps[hf * 64:(hf + 1) * 64, 4, 2 * i:2 * i + 2], a[:, c:c + 64], ones[:, 0:2],
                                            start=(a is acc), stop=(a is R))
            last.then_inc(fin_pe, 1)
            pe.wait_ge(xf_ready, KT)
            pe.wait_ge(ps_free[0], N_SLABS // 2 + 1)
            pe.wait_ge(ps_free[1], N_SLABS // 2)
            for i in range(5):
                cols = slice(0, TS) if i == 0 else slice(TS + (i - 1) * P, TS + i * P)
                n = cols.stop - cols.start
                if i >= 3:
                    pe.wait_ge(y_act, i - 2)
                    pe.wait_ge(y_dve, i - 2)
                for k in range(KT):
                    last = nc.tensor.transpose(ps[0:n, YB[i] + k // 4, k % 4 * P:(k % 4 + 1) * P], xf[:, k, cols], ident[:])
                last.then_inc(yt_done, 1)


_INS = ['x_prompt', 'x_sample', 'state_mlstm_C', 'state_mlstm_n', 'state_mlstm_m', 'state_s5_re', 'state_s5_im',
        'norm_mix_g', 'norm_ffn_g', 'norm_final_g', 'mlstm_w_in', 'mlstm_b_i', 'mlstm_b_f', 'mlstm_head_norm_g',
        'mlstm_w_out', 's5_lambda_re', 's5_lambda_im', 's5_log_dt', 's5_b_re', 's5_b_im', 's5_c_re', 's5_c_im',
        's5_d', 's5_w_glu', 'ffn_w_up', 'ffn_w_down']
_OUTS = [(1, L, D), (B, T, D), (1, 1, H, DK, DV), (1, 1, H, DK), (1, 1, H), (1, 1, G, SP), (1, 1, G, SP),
         (1, B, H, DK, DV), (1, B, H, DK), (1, B, H), (1, B, G, SP), (1, B, G, SP)]


def kernel(**inputs):
    import concourse.bacc as _bacc
    from concourse.bass_utils import run_bass_kernel_spmd as _run

    nc = _bacc.Bacc("TRN2", target_bir_lowering=False, num_devices=1)
    arrays, args = {}, []
    for name in _INS:
        a = np.ascontiguousarray(inputs[name])
        arrays[f"in_{name}"] = a
        args.append(nc.dram_tensor(f"in_{name}", a.shape, mybir.dt.from_np(a.dtype), kind="ExternalInput").ap())
    for i, shape in enumerate(_OUTS):
        args.append(nc.dram_tensor(f"out_{i}", shape, F32, kind="ExternalOutput").ap())
    build(nc, *args)
    r = _run(nc, [arrays], core_ids=[0])
    return tuple(r.results[0][f"out_{i}"] for i in range(len(_OUTS)))
```
